# Optimizing a Trainium2 kernel written in Bass

```python
import math, functools
import jax, jax.numpy as jnp
from jax import lax
import numpy as np

D_MODEL = 1024
BATCH = 1
SEQ = 1024
DEPTH = 1
DEC_BATCH = 8
DEC_SEQ = 4
PAST_LEN = 2048
PAGE_SIZE = 128

N_HEADS = 8
HEAD_DIM = 64
ATT_WIDTH = N_HEADS * HEAD_DIM
CONV_GROUPS = 8
CONV_GROUP_CH = 64
CONV_CH = CONV_GROUPS * CONV_GROUP_CH
CONV_WIDTH = 3
D_FF = 4 * D_MODEL
Q_BLOCK = 128
EPS = 1e-6
N_MOD = 6
SB_SCALE = 1.0 / math.sqrt(HEAD_DIM)
SB_BIAS_INIT = -8.0
IN_SPLITS = (ATT_WIDTH,) * 3 + (CONV_CH,) * 3 + (D_MODEL,) * 2
IN_WIDTH = sum(IN_SPLITS)
IN_OFFSETS = np.cumsum(IN_SPLITS)[:-1].tolist()

kernel_name = "stickbreak_shortconv_gated_hybrid_step"

def rms_norm(x, g):
    x32 = x.astype(jnp.float32)
    y = x32 * lax.rsqrt(jnp.mean(x32 * x32, axis=-1, keepdims=True) + EPS)
    return (y * g.astype(jnp.float32)).astype(x.dtype)

def ada_mod(c, w_ada, b_ada):
    m = jax.nn.silu(c) @ w_ada + b_ada
    return [t[:, None, :] for t in jnp.split(m, N_MOD, axis=-1)]

def project_in(h, w_in, q_norm_g, k_norm_g):
    b, t, _ = h.shape
    parts = jnp.split(h @ w_in, IN_OFFSETS, axis=-1)
    q = rms_norm(parts[0].reshape(b, t, N_HEADS, HEAD_DIM), q_norm_g)
    k = rms_norm(parts[1].reshape(b, t, N_HEADS, HEAD_DIM), k_norm_g)
    v = parts[2].reshape(b, t, N_HEADS, HEAD_DIM)
    return q, k, v, parts[3], parts[4], parts[5], parts[6], parts[7]

def stick_breaking(z, valid):
    log_beta = jax.nn.log_sigmoid(z)
    log_keep = jnp.where(valid, jax.nn.log_sigmoid(-z), 0.0)
    suffix = lax.cumsum(log_keep, axis=z.ndim - 1, reverse=True) - log_keep
    return jnp.where(valid, jnp.exp(log_beta + suffix), 0.0)

def sb_logits(q, k, sb_bias):
    z = jnp.einsum('bqhd,bkhd->bhqk', q, k).astype(jnp.float32) * SB_SCALE
    return z + sb_bias.astype(jnp.float32)[None, :, None, None]

def sb_attention_prompt(q, k, v, sb_bias):
    b, t, h, d = q.shape
    key_pos = jnp.arange(t)

    def block(i):
        start = i * Q_BLOCK
        qb = lax.dynamic_slice_in_dim(q, start, Q_BLOCK, axis=1)
        z = sb_logits(qb, k, sb_bias)
        q_pos = start + jnp.arange(Q_BLOCK)
        valid = key_pos[None, :] < q_pos[:, None]
        a = stick_breaking(z, valid).astype(v.dtype)
        return jnp.einsum('bhqk,bkhd->bqhd', a, v)

    o = lax.map(block, jnp.arange(t // Q_BLOCK))
    return jnp.moveaxis(o, 0, 1).reshape(b, t, h, d)

def sb_attention_sample(q, k_new, v_new, sb_bias, k_past, v_past):
    p = k_past.shape[1]
    t = q.shape[1]
    z = jnp.concatenate([sb_logits(q, k_past, sb_bias), sb_logits(q, k_new, sb_bias)], axis=-1)
    key_pos = jnp.arange(p + t)
    q_pos = p + jnp.arange(t)
    valid = key_pos[None, :] < q_pos[:, None]
    a = stick_breaking(z, valid).astype(v_new.dtype)
    return (jnp.einsum('bhqk,bkhd->bqhd', a[..., :p], v_past)
            + jnp.einsum('bhqk,bkhd->bqhd', a[..., p:], v_new))

def short_conv(u, prev, w, bias):
    t = u.shape[1]
    win = jnp.concatenate([prev.astype(u.dtype), u], axis=1)
    y = bias + sum(w[j] * win[:, j:j + t] for j in range(CONV_WIDTH))
    return y, win[:, -(CONV_WIDTH - 1):]

def merge_branches(o_att, y_conv, ga, gb, w_att_out, w_conv_out, w_o):
    b, t = y_conv.shape[:2]
    ya = o_att.reshape(b, t, ATT_WIDTH) @ w_att_out
    yb = y_conv @ w_conv_out
    return (jax.nn.sigmoid(ga) * ya + jax.nn.sigmoid(gb) * yb) @ w_o

def sqrelu_mlp(h, w1, w2):
    return jnp.square(jax.nn.relu(h @ w1)) @ w2

def decoder_layer(x, c, attend, conv_prev, rms_g1, rms_g2, w_ada, b_ada, w_in, q_norm_g, k_norm_g, sb_bias,
                  conv_w, conv_b, w_att_out, w_conv_out, w_o, w_mlp1, w_mlp2):
    sh1, sc1, gt1, sh2, sc2, gt2 = ada_mod(c, w_ada, b_ada)
    h = rms_norm(x, rms_g1) * (1 + sc1) + sh1
    q, k, v, hc, bgate, cgate, ga, gb = project_in(h, w_in, q_norm_g, k_norm_g)
    o_att = attend(q, k, v, sb_bias)
    yc, conv_state = short_conv(cgate * hc, conv_prev, conv_w, conv_b)
    x = x + gt1 * merge_branches(o_att, bgate * yc, ga, gb, w_att_out, w_conv_out, w_o)
    h2 = rms_norm(x, rms_g2) * (1 + sc2) + sh2
    x = x + gt2 * sqrelu_mlp(h2, w_mlp1, w_mlp2)
    return x, k, v, conv_state

def setup_inputs(seed: int = 0) -> dict:
    key = jax.random.key(seed)
    ks = jax.random.split(key, 24)
    n_pages = PAST_LEN // PAGE_SIZE
    n_used = DEC_BATCH * n_pages
    n_phys = n_used + max(1, n_used // 4)
    f32 = jnp.float32
    nrm = lambda k, s, scale: jax.random.normal(k, s, f32) * scale
    page_table = jax.random.permutation(ks[7], n_phys)[:n_used].reshape(DEC_BATCH, n_pages).astype(jnp.int32)
    return {
        "x_prompt": nrm(ks[0], (BATCH, SEQ, D_MODEL), 1.0),
        "x_sample": nrm(ks[1], (DEC_BATCH, DEC_SEQ, D_MODEL), 1.0),
        "c_prompt": nrm(ks[2], (BATCH, D_MODEL), 1.0),
        "c_sample": nrm(ks[3], (DEC_BATCH, D_MODEL), 1.0),
        "cache_k": nrm(ks[4], (DEPTH, n_phys, PAGE_SIZE, N_HEADS, HEAD_DIM), 1.0),
        "cache_v": nrm(ks[5], (DEPTH, n_phys, PAGE_SIZE, N_HEADS, HEAD_DIM), 1.0),
        "state_conv": nrm(ks[6], (DEPTH, DEC_BATCH, CONV_WIDTH - 1, CONV_CH), 1.0),
        "page_table": page_table,
        "rms_g1": 1.0 + nrm(ks[8], (DEPTH, D_MODEL), 0.02),
        "rms_g2": 1.0 + nrm(ks[9], (DEPTH, D_MODEL), 0.02),
        "w_ada": nrm(ks[10], (DEPTH, D_MODEL, N_MOD * D_MODEL), 0.2 * D_MODEL ** -0.5),
        "b_ada": nrm(ks[11], (DEPTH, N_MOD * D_MODEL), 0.01),
        "w_in": nrm(ks[12], (DEPTH, D_MODEL, IN_WIDTH), D_MODEL ** -0.5),
        "q_norm_g": 1.0 + nrm(ks[13], (DEPTH, HEAD_DIM), 0.02),
        "k_norm_g": 1.0 + nrm(ks[14], (DEPTH, HEAD_DIM), 0.02),
        "sb_bias": SB_BIAS_INIT + nrm(ks[22], (DEPTH, N_HEADS), 0.1),
        "conv_w": nrm(ks[15], (DEPTH, CONV_WIDTH, CONV_CH), CONV_WIDTH ** -0.5),
        "conv_b": nrm(ks[16], (DEPTH, CONV_CH), 0.01),
        "w_att_out": nrm(ks[17], (DEPTH, ATT_WIDTH, D_MODEL), ATT_WIDTH ** -0.5),
        "w_conv_out": nrm(ks[18], (DEPTH, CONV_CH, D_MODEL), CONV_CH ** -0.5),
        "w_o": nrm(ks[19], (DEPTH, D_MODEL, D_MODEL), D_MODEL ** -0.5),
        "w_mlp1": nrm(ks[20], (DEPTH, D_MODEL, D_FF), D_MODEL ** -0.5),
        "w_mlp2": nrm(ks[21], (DEPTH, D_FF, D_MODEL), D_FF ** -0.5),
    }

def reference(x_prompt, x_sample, c_prompt, c_sample, cache_k, cache_v, state_conv, page_table,
              rms_g1, rms_g2, w_ada, b_ada, w_in, q_norm_g, k_norm_g, sb_bias, conv_w, conv_b,
              w_att_out, w_conv_out, w_o, w_mlp1, w_mlp2):
    yp, ys = x_prompt, x_sample
    bp, bs = x_prompt.shape[0], x_sample.shape[0]
    kp_l, vp_l, cp_l, ks_l, vs_l, cs_l = [], [], [], [], [], []
    for l in range(DEPTH):
        lw = (rms_g1[l], rms_g2[l], w_ada[l], b_ada[l], w_in[l], q_norm_g[l], k_norm_g[l], sb_bias[l],
              conv_w[l], conv_b[l], w_att_out[l], w_conv_out[l], w_o[l], w_mlp1[l], w_mlp2[l])
        conv0 = jnp.zeros((bp, CONV_WIDTH - 1, CONV_CH), yp.dtype)
        yp, kp, vp, cp = decoder_layer(yp, c_prompt, sb_attention_prompt, conv0, *lw)
        k_past = cache_k[l][page_table].reshape(bs, -1, N_HEADS, HEAD_DIM)
        v_past = cache_v[l][page_table].reshape(bs, -1, N_HEADS, HEAD_DIM)
        attend = functools.partial(sb_attention_sample, k_past=k_past, v_past=v_past)
        ys, kn, vn, cn = decoder_layer(ys, c_sample, attend, state_conv[l], *lw)
        kp_l.append(kp); vp_l.append(vp); cp_l.append(cp)
        ks_l.append(kn); vs_l.append(vn); cs_l.append(cn)
    return (yp, ys, jnp.stack(kp_l), jnp.stack(vp_l), jnp.stack(cp_l),
            jnp.stack(ks_l), jnp.stack(vs_l), jnp.stack(cs_l))


_drawn_inputs = setup_inputs


def setup_inputs(seed=0):
    import zlib

    import numpy as np

    out = dict(_drawn_inputs(seed))
    spreads = {}
    factors = {'cache_k': 8.0,
     'cache_v': 8.0,
     'rms_g2': 8.0,
     'b_ada': 2.856,
     'q_norm_g': 8.0,
     'k_norm_g': 2.93,
     'sb_bias': 8.0,
     'conv_b': 64.0,
     'w_att_out': 8.0,
     'state_conv': 5.905}
    for name, (base, spread) in spreads.items():
        noise = np.random.default_rng([zlib.crc32(name.encode()), seed]).standard_normal(out[name].shape)
        drawn = base * np.exp(spread * noise) if base else spread * noise
        out[name] = __import__('jax').numpy.asarray(drawn.astype(out[name].dtype))
    for name, factor in factors.items():
        out[name] = (out[name] * factor).astype(out[name].dtype)
    return out
```

```python
from contextlib import ExitStack

import numpy as np
import concourse.bass as bass
from concourse import mybir

F32 = mybir.dt.float32
F32R = mybir.dt.float32r
I32 = mybir.dt.int32
ALU = mybir.AluOpType
ACT = mybir.ActivationFunctionType
AX = mybir.AxisListType
ds = bass.ds

P = 128
D = 1024
SEQ = 1024
DEC_B = 8
DEC_T = 4
NS = DEC_B * DEC_T
T = SEQ + NS
NCH = 3
CH = T // NCH
LASTP = SEQ - 2 * CH
HD = 64
NH = 8
NPAIR = NH // 2
ATT = NH * HD
CONV = 512
CB = CONV // P
FF = 4096
DB = D // P
PAGES = 16
PAGE = 128
NPHYS = 160
EPS = 1e-6
BIG = 3.0e38
NEG = -1.0e30
UC = 256
NMOD = 6
CREDIT = 2
CREDIT4 = 4
N_SMALL = 14


class Chain:

    def __init__(self, eng, sem):
        self.eng, self.sem, self.n, self.i, self.per, self.k = eng, sem, 0, None, 0, 0

    def did(self, inst):
        inst.then_inc(self.sem, 1)
        self.k += 1

    def sync(self):
        at = self.n + self.k
        self.eng.wait_ge(self.sem, at if self.i is None else self.i * self.per + at)

    def enter(self, i, per):
        self.n, self.k, self.i, self.per = self.n + self.k, 0, i, per

    def leave(self, trips):
        assert self.k == self.per, f"a loop of {self.k} steps, declared {self.per}"
        self.n, self.k, self.i = self.n + trips * self.per, 0, None


PHASES = {}


def plan():
    g = vd = va = CREDIT
    vd = va = CREDIT
    for name, trips, pattern in (
        ("ada", 12, "dd"),
        ("qk", 2, "d" * 12),
        ("v", 1, "d" * 18),
        ("conv", 4, "d" * 9 + "aaa"),
        ("gates", 3, "a" * 12),
        ("mix", 2, "d" * 24),
        ("wo", 2, "d" * 12),
        ("mlp", 8, "a" * 12 + "d" * 24),
    ):
        PHASES[name] = (g, vd, va, trips, pattern)
        g += trips * len(pattern)
        vd += trips * pattern.count("d")
        va += trips * pattern.count("a")


plan()


def steps_of_pair():
    return [(qc, j, h) for qc in (0, 1) for j in range(4 * qc + 3, -1, -1) for h in (0, 1)]


STEPS = steps_of_pair()
NSTEP = len(STEPS)
LATE_SOFTPLUS, LATE_SUMS, LATE_REST, LATE_PROB, LATE_VALUES, LATE_OUT = 1, 3, 4, 4, 6, 7
AV_CREDIT = 8


def step_of(k):
    qc, j, h = STEPS[k % NSTEP]
    return qc, j, h, max(0, P * j - 512 * qc), j >= 4 * qc


def program(nc, a):
    ctx = ExitStack()
    with ctx:
        def sem(name):
            return ctx.enter_context(nc.semaphore(name))

        here = [16512]

        def put(name, shape, dt, at=None):
            size = int(np.prod(shape[1:])) * 4
            if at is None:
                at = here[0]
                here[0] += (size + 63) // 64 * 64
            assert at + size <= 229344, name
            return nc.alloc_sbuf_tensor_at(name, shape, dt, offset=at)

        ident = put("ident", [P, P], F32)
        ones = put("ones", [P, P], F32)
        headones = put("headones", [P, P], F32)
        diagcap = put("diagcap", [P, P], F32)
        suffix_r = put("suffix_r", [P, P], F32R)
        prefix_r = put("prefix_r", [P, P], F32R)
        ones_r = put("ones_r", [P, P], F32R)
        newcap = put("newcap", [DEC_T, NH, DEC_T], F32)
        sel9 = put("sel9", [18, 9], F32)
        sel4 = put("sel4", [2 * NH * DEC_T, DEC_T], F32)
        eps = put("eps", [P, 1], F32)
        zero = put("zero", [P, 1], F32)
        mods = put("mods", [P, NMOD * DB, 9], F32)
        vec = put("vec", [P, 82], F32)
        gqk = put("gqk", [P, 8], F32)
        hist = put("hist", [P, CB, 16], F32)
        bias8 = put("bias8", [P, NH], F32)
        headrow = put("headrow", [2 * NH * DEC_T, NH], F32)
        tail = put("tail", [P, CB, 18], F32)
        pages = put("pages", [1, DEC_B * PAGES], I32)
        qks = put("qks", [P, DB, NS], F32)
        vnew = put("vnew", [DEC_T, ATT], F32)
        raw = [put(f"raw{s}", [P, 2048], F32) for s in (0, 1)]
        wh = [put(f"wh{s}", [P, 2048], F32R) for s in (0, 1)]
        wl = [put(f"wl{s}", [P, 2048], F32R) for s in (0, 1)]
        BLK = T * 4
        base = here[0]

        def blk(name, b, shape, dt, extra=0):
            return put(name, shape, dt, at=base + b * BLK + extra)

        xload = blk("xload", 0, [P, 9, D], F32)
        vecrow = blk("vecrow", 9, [82, P], F32)
        histrow = blk("histrow", 9, [16, CONV], F32, 512)
        crow = blk("crow", 10, [9, D], F32)
        csig = blk("csig", 11, [9, D], F32)
        sfx_f = blk("sfx_f", 12, [P, P], F32)
        pfx_f = blk("pfx_f", 12, [P, P], F32, 512)
        chl = blk("chl", 13, [P, DB, 18], F32R)
        adaY = [blk(f"adaY{s}", 14, [18, UC], F32, 1024 * s) for s in (0, 1)]
        hH = blk("hH", 0, [P, DB, T], F32R)
        hL = blk("hL", 8, [P, DB, T], F32R)
        act8 = blk("act8", 16, [P, DB, T], F32)
        vsb = blk("vsb", 24, [P, 9, ATT], F32)
        us = blk("us", 24, [P, DEC_B, 6], F32, 18432)
        sq = [blk(f"sq{s}", 29, [P, CH], F32, 1408 * s) for s in (0, 1)]
        rstd = blk("rstd", 30, [P, T], F32)
        nrm = [blk(f"nrm{s}", 31 + s, [P, T], F32) for s in (0, 1)]
        hF = [blk(f"hF{s}", 33 + s, [P, T], F32) for s in (0, 1)]
        qsq = [blk(f"qsq{s}", 29 + s, [P, T], F32) for s in (0, 1)]
        qrs = [blk(f"qrs{s}", 31 + s, [P, T], F32) for s in (0, 1)]
        kout = [blk(f"kout{s}", 33 + s, [P, ATT], F32) for s in (0, 1)]
        gt = [blk(f"gt{s}", 29 + s, [P, T], F32) for s in (0, 1)]
        hcs = gt[1]
        up = blk("up", 31, [P, 2 + SEQ], F32)
        yc = blk("yc", 32, [P, CB, T], F32)
        tailT = blk("tailT", 31, [18, CONV], F32)
        kh = blk("kh", 0, [P, SEQ], F32R)
        kl = blk("kl", 0, [P, SEQ], F32R, 4096)
        qh = blk("qh", 0, [P, SEQ], F32R, 8192)
        ql = blk("ql", 0, [P, SEQ], F32R, 12288)
        zb = [blk(f"zb{s}", 0, [P, 512], F32, 16384 + 2048 * s) for s in range(6)]
        tl = [blk(f"tl{s}", 0, [P, 512], F32, 28672 + 2048 * s) for s in range(3)]
        sh = [blk(f"sh{s}", 0, [P, 512], F32R, 34816 + 2048 * s) for s in range(4)]
        prob = [blk(f"prob{s}", 0, [P, 512], F32, 43008 + 2048 * s) for s in range(3)]
        sp_ = [blk(f"sp{s}", 29, [P, 512], F32, 2048 * s) for s in range(3)]
        ph = [blk(f"ph{s}", 29, [P, 512], F32R, 6144 + 2048 * s) for s in range(3)]
        sl = [wh[0][:, 512 * s:512 * s + 512] for s in range(4)]
        pl = [wh[1][:, 512 * s:512 * s + 512] for s in range(3)]
        vcH, vcL = (wl[0][:, at:at + SEQ].rearrange("p (t d) -> p t d", t=8) for at in (0, SEQ))
        oF = blk("oF", 12, [P, NPAIR, T], F32)
        kraw = [blk(f"kraw{s}", 16, [P, 4, ATT], F32, 8192 * s) for s in range(4)]
        vh = [wh[0], wh[1]] + [blk(f"vh{s}", 0, [P, 2048], F32R, 8192 * (s - 2)) for s in (2, 3)]
        vl = [wl[0], wl[1]] + [blk(f"vl{s}", 0, [P, 2048], F32R, 8192 * s) for s in (2, 3)]
        kTh = blk("kTh", 0, [P, 4, 512], F32R, 32768)
        kTl = blk("kTl", 0, [P, 4, 512], F32R, 40960)
        DP = PAGES + 1
        dnext = [0]

        def dec(name, shape, dt):
            size = int(np.prod(shape[1:])) * 4
            t = blk(name, 24, shape, dt, dnext[0])
            dnext[0] += (size + 63) // 64 * 64
            assert dnext[0] <= 8 * BLK
            return t

        ROWS = NH * DEC_T
        dzb = dec("dzb", [P, DP, ROWS], F32)
        dpr = dec("dpr", [P, DP, ROWS], F32)
        dtl = dec("dtl", [P, DP, ROWS], F32)
        dcar = dtl
        dsp = dec("dsp", [P, DP, ROWS], F32)
        dsh = dec("dsh", [P, DP, ROWS], F32R)
        dsl = dec("dsl", [P, DP, ROWS], F32R)
        dch = dec("dch", [P, PAGES, ROWS], F32R)
        dcl = dec("dcl", [P, PAGES, ROWS], F32R)
        dp2 = dec("dp2", [P, DP, 2 * ROWS], F32R)
        headmask = dec("headmask", [2 * ROWS, NH, HD], F32)
        osel = dec("osel", [2 * ROWS, ATT], F32)
        vnewH = dec("vnewH", [DEC_T, ATT], F32R)
        vnewL = dec("vnewL", [DEC_T, ATT], F32R)
        qbF = blk("qbF", 0, [P, 5 * ROWS], F32, 49152)
        qbh = blk("qbh", 0, [P, 5 * ROWS], F32R, 49152 + 640)
        qbl = dec("qbl", [P, 5 * ROWS], F32R)
        zrow = dec("zrow", [ROWS, 512], F32)
        zrow_new = dec("zrow_new", [ROWS, DEC_T], F32)
        knh = dec("knh", [P, NPAIR, DEC_T], F32R)
        knl = dec("knl", [P, NPAIR, DEC_T], F32R)
        bias32 = dec("bias32", [P, NH, DEC_T], F32)
        oH = blk("oH", 16, [P, NPAIR, T], F32R)
        oL = blk("oL", 20, [P, NPAIR, T], F32R)
        ycH = blk("ycH", 24, [P, CB, T], F32R)
        ycL = blk("ycL", 28, [P, CB, T], F32R)
        ga = [blk(f"ga{s}", 32 + 2 * s, [P, T], F32) for s in (0, 1)]
        gb = [blk(f"gb{s}", 33 + 2 * s, [P, T], F32) for s in (0, 1)]
        mixH = blk("mixH", 0, [P, DB, T], F32R)
        mixL = blk("mixL", 8, [P, DB, T], F32R)
        x1 = blk("x1", 24, [P, DB, T], F32)
        h2H = blk("h2H", 0, [P, DB, T], F32R)
        h2L = blk("h2L", 8, [P, DB, T], F32R)
        sq2 = [blk(f"sq2{s}", 16, [P, CH], F32, 1408 * s) for s in (0, 1)]
        rstd2 = blk("rstd2", 17, [P, T], F32)
        nrm2 = [blk(f"nrm2{s}", 18 + s, [P, T], F32) for s in (0, 1)]
        hF2 = [blk(f"hF2{s}", 20 + s, [P, T], F32) for s in (0, 1)]
        hidH = blk("hidH", 16, [P, 4, T], F32R)
        hidL = blk("hidL", 20, [P, 4, T], F32R)
        rel = [blk(f"rel{s}", 32, [P, CH], F32, 1408 * s) for s in (0, 1)]
        rsq = [blk(f"rsq{s}", 33, [P, CH], F32, 1408 * s) for s in (0, 1)]
        smp = [blk(f"smp{s}", 34, [P, NS], F32, 128 * s) for s in (0, 1)]
        yrow = [blk(f"yrow{s}", 2 * s, [P, D], F32) for s in (0, 1)]

        bank = [ctx.enter_context(nc.psum_tensor(f"bank{b}", [P, 512], F32)) for b in range(8)]
        LIN = (6, 7)

        x_dram = nc.dram_tensor("x_scratch", (DB, P, T), F32).ap()
        gate_dram = nc.dram_tensor("gate_scratch", (16, P, T), F32).ap()

        S = {n: sem(n) for n in """
            small_in x_in raw_in0 raw_in1 consts pool_step split products bank_dve bank_act dve_step act_step
            c_ready c_turned vec_turned c_split ada_sel mods_in mods_ready x_turned xT_act xT_dve x_saved
            squares square_sum mean_read rstd_ready normed scaled_act scaled_dve h_hi h_lo
            qk_square qk_sum qk_rstd qk_ready v_out kturned kout_ready kout_dma0 kout_dma1
            kout_free gate_exp gate_ready gate_dma0 gate_dma1 yc_ready tail_turned tail_ready tail_dma
            qk_hi pair_ready values_hi values_ready z_done zb_done absz log_done sp_done sp_hi sp_lo tri_done arg_done prob_done prob_hi prob_lo av_done o_out
            q_saved k_in0 k_in1 k_in2 k_in3 v_in0 v_in1 vnew_in v_hi v_lo vnew_hi vnew_lo kt_done kt_hi kt_lo z_used znew_done zrow_ready dz_done dabs dlog dsp_done dsp_hi
            dsum_ready ds_done darg dprob dprob_lo d_av q_block d_osel d_otr d_oout
            oy_hi oy_lo gates_in0 gates_in1 mix_done mix_hi mix_lo x_back x1_ready relu_done sq_done hid_hi hid_lo
            acc_done y_turned y_act y_dve y_dma0 y_dma1
        """.split()}

        def w_in(n):
            return S[f"raw_in{n}"]

        block = ctx.enter_context(nc.Block())

        win = a["w_in"][0].rearrange("(k p) n -> p k n", p=P)
        wada = a["w_ada"][0].rearrange("(k p) n -> p k n", p=P)
        wo = a["w_o"][0].rearrange("(k p) n -> p k n", p=P)
        wao = a["w_att_out"][0].rearrange("(k p) n -> p k n", p=P)
        wco = a["w_conv_out"][0].rearrange("(k p) n -> p k n", p=P)
        w1 = a["w_mlp1"][0].rearrange("(k p) n -> p k n", p=P)
        w2 = a["w_mlp2"][0].rearrange("(g k p) n -> g p k n", k=4, p=P)
        ck = a["cache_k"][0].rearrange("g t h d -> g t (h d)")
        cv = a["cache_v"][0].rearrange("g t h d -> g t (h d)")
        O_HC, O_B, O_C, O_GA = 3 * ATT, 3 * ATT + CONV, 3 * ATT + 2 * CONV, 3 * ATT + 3 * CONV

        @block.sync
        def _(sp):
            unit = [0]

            def load_unit(s, n, halves):
                if not (isinstance(n, int) and n < 2):
                    sp.wait_ge(S["split"], n - 1)
                for dst, src in halves:
                    sp.dma_start(dst, src).then_inc(w_in(s), 16)

            def cols(s, w, col):
                v = raw[s][:, :].rearrange("p (k n) -> p k n", k=8)
                return [(v[:, 4 * h:4 * h + 4, :], w[:, 4 * h:4 * h + 4, ds(col, UC)]) for h in (0, 1)]

            def two_cols(s, w, col0, col1):
                v = raw[s][:, :].rearrange("p (k n) -> p k n", k=8)
                return [(v[:, :, 0:P], w[:, :, ds(col0, P)]), (v[:, :, P:UC], w[:, :, ds(col1, P)])]

            def stream(trips, per, units):
                with sp.Fori(0, trips) as i:
                    for u in range(per):
                        load_unit(u % 2, i * per + (unit[0] + u), units(i, u))
                unit[0] += trips * per

            def ada_unit(i, u):
                return cols(u, wada, i * (2 * UC) + u * UC)

            small = [
                (vecrow[0:48, :], a["b_ada"][0].rearrange("(r c) -> r c", c=P)),
                (vecrow[48:56, :], a["rms_g1"][0].rearrange("(r c) -> r c", c=P)),
                (vecrow[56:64, :], a["rms_g2"][0].rearrange("(r c) -> r c", c=P)),
                (vecrow[64:76, :], a["conv_w"][0].rearrange("j (r c) -> (j r) c", c=P)),
                (vecrow[76:80, :], a["conv_b"][0].rearrange("(r c) -> r c", c=P)),
                (vecrow[80:81, 0:HD], a["q_norm_g"][0:1, :]),
                (vecrow[80:81, HD:P], a["q_norm_g"][0:1, :]),
                (vecrow[81:82, 0:HD], a["k_norm_g"][0:1, :]),
                (vecrow[81:82, HD:P], a["k_norm_g"][0:1, :]),
                (histrow[:, :], a["state_conv"][0].rearrange("b j c -> (b j) c")),
                (crow[0:1, :], a["c_prompt"]),
                (crow[1:9, :], a["c_sample"]),
                (bias8[:, :], a["sb_bias"][0].partition_broadcast(P)),
                (pages[:, :], a["page_table"].rearrange("(o b) g -> o (b g)", o=1)),
            ]
            for dst, src in small:
                sp.dma_start(dst, src).then_inc(S["small_in"], 16)
            assert len(small) == N_SMALL
            for u in (0, 1):
                load_unit(u, u, cols(u, wada, u * UC))
            sp.dma_start(xload[:, 0:8, :], a["x_prompt"][0].rearrange("(t p) d -> p t d", p=P)).then_inc(S["x_in"], 16)
            sp.dma_start(xload[0:NS, 8, :], a["x_sample"].rearrange("b t d -> (b t) d")).then_inc(S["x_in"], 16)
            unit[0] = 2
            stream(11, 2, lambda i, u: cols(u, wada, i * (2 * UC) + (2 + u) * UC))
            stream(2, 2, lambda i, u: cols(u, win, i * (2 * UC) + u * UC))
            stream(1, 2, lambda i, u: cols(u, win, 2 * ATT + u * UC))
            stream(4, 2, lambda i, u: two_cols(u, win, i * P + (O_B if u else O_HC), i * P + (O_GA if u else O_C)))
            stream(3, 2, lambda i, u: cols(u, win, i * (2 * UC) + (O_GA + CONV + u * UC)))

            def merge_unit(i, u):
                v = raw[u][:, :].rearrange("p (k n) -> p k n", k=8)
                at = i * (2 * UC) + u * UC
                return [(v[:, 0:4, :], wao[:, :, ds(at, UC)]), (v[:, 4:8, :], wco[:, :, ds(at, UC)])]

            def page_numbers(b, c):
                return [sp.value_load(pages[0:1, ds(b * PAGES + (4 * c + g), 1)], min_val=0, max_val=NPHYS - 1)
                        for g in range(4)]

            def load_k(b, c):
                numbers = page_numbers(b, c)
                if not isinstance(b, int):
                    sp.wait_ge(S["kt_done"], 16 * b + (4 * (c + 1) - 16 + CREDIT))
                for g, page in enumerate(numbers):
                    sp.dma_start(kraw[c][:, g, :], ck[page, :, :]).then_inc(S[f"k_in{c}"], 16)

            def load_v(b, c):
                numbers = page_numbers(b, c)
                if not (isinstance(b, int) and b == 0 and c < 2):
                    sp.wait_ge(S["v_lo"], 4 * b + (c - 1))
                dst = raw[c % 2][:, :].rearrange("p (g c) -> p g c", g=4)
                for g, page in enumerate(numbers):
                    sp.dma_start(dst[:, g, :], cv[page, :, :]).then_inc(S[f"v_in{c % 2}"], 16)

            def load_new_v(b):
                if not (isinstance(b, int) and b == 0):
                    sp.wait_ge(S["vnew_lo"], b)
                sp.dma_start(vnew[:, :], a["v_sample"][0, b].rearrange("t h d -> t (h d)")).then_inc(S["vnew_in"], 16)

            sp.wait_ge(S["split"], unit[0])
            for c in (0, 1):
                load_v(0, c)
            sp.wait_ge(S["v_out"], 32)
            load_new_v(0)
            sp.wait_ge(S["pair_ready"], NPAIR)
            sp.wait_ge(S["q_saved"], 1)
            for c in range(4):
                load_k(0, c)
            with sp.Fori(1, DEC_B) as b:
                load_k(b, 0)
                load_k(b, 1)
                load_k(b, 2)
                load_v(b - 1, 2)
                load_k(b, 3)
                load_v(b - 1, 3)
                load_v(b, 0)
                load_v(b, 1)
                load_new_v(b)
            for c in (2, 3):
                load_v(DEC_B - 1, c)
            sp.wait_ge(S["v_lo"], 4 * DEC_B)
            for u in (0, 1):
                load_unit(u, unit[0] + u, merge_unit(0, u))

            sp.wait_ge(S["oy_lo"], 2)
            sp.wait_ge(S["gate_dma0"], 16 * 10 + 16)
            sp.wait_ge(S["gate_dma1"], 16 * 6 + 16)
            gin = (S["gates_in0"], S["gates_in1"])

            def load_gates(i, u):
                for m in (0, 1):
                    b = i * 4 + (2 * u + m)
                    sp.wait_ge(S["mix_lo"], 12 * i + (3 * (2 * u + m - 1) + 3 * CREDIT))
                    sp.dma_start(ga[m][:, :], gate_dram[ds(b, 1), :, :].rearrange("o p t -> (o p) t")).then_inc(gin[m], 16)
                    sp.dma_start(gb[m][:, :], gate_dram[ds(b + DB, 1), :, :].rearrange("o p t -> (o p) t")).then_inc(gin[m], 16)

            for u in (0, 1):
                load_gates(0, u)
            for u in (0, 1):
                load_unit(u, unit[0] + 2 + u, merge_unit(1, u))
                load_gates(1, u)
            unit[0] += 4
            stream(2, 2, lambda i, u: cols(u, wo, i * (2 * UC) + u * UC))

            def mlp_unit(i, u):
                if u < 2:
                    return cols(u, w1, i * (2 * UC) + u * UC)
                v = raw[u % 2][:, :].rearrange("p (k n) -> p k n", k=4)
                return [(v[:, 2 * h:2 * h + 2, :],
                         w2[ds(i, 1), :, 2 * h:2 * h + 2, (u - 2) * 512:(u - 1) * 512].rearrange("o p k n -> (o p) k n"))
                        for h in (0, 1)]

            stream(8, 4, mlp_unit)

            yout = (S["y_dma0"], S["y_dma1"])
            for t in range(9):
                sp.wait_ge(S["y_act"], t + 1)
                sp.wait_ge(S["y_dve"], t + 1)
                if t < 8:
                    sp.dma_start(a["y_prompt"][0, t * P:(t + 1) * P, :], yrow[t % 2][:, :]).then_inc(yout[t % 2], 16)
                else:
                    sp.dma_start(a["y_sample"].rearrange("b t d -> (b t) d"), yrow[0][0:NS, :]).then_inc(yout[0], 16)
            sp.wait_ge(S["y_dma0"], 5 * 16)
            sp.wait_ge(S["y_dma1"], 4 * 16)
            sp.wait_ge(S["kout_dma0"], 5 * 16)
            sp.wait_ge(S["kout_dma1"], 4 * 16)
            sp.wait_ge(S["v_out"], 2 * 16)
            sp.wait_ge(S["tail_dma"], 2 * 16)
            sp.wait_ge(S["x_saved"], 16)

        @block.gpsimd
        def _(pool):
            ch = Chain(pool, S["pool_step"])

            def fill(t, value):
                ch.did(pool.memset(t, value))
                ch.sync()

            def keep(t, cmp, fillv, base_, pattern, cm):
                ch.did(pool.affine_select(out=t, in_=t, compare_op=cmp, fill=fillv, base=base_, pattern=pattern,
                                          channel_multiplier=cm))
                ch.sync()

            fill(ident[:, :], 0.0)
            keep(ident[:, :], ALU.not_equal, 1.0, 0, [[-1, P]], 1)
            fill(ones[:, :], 1.0)
            fill(sfx_f[:, :], 1.0)
            keep(sfx_f[:, :], ALU.is_ge, 0.0, 0, [[-1, P]], 1)
            fill(pfx_f[:, :], 1.0)
            keep(pfx_f[:, :], ALU.is_gt, 0.0, 0, [[1, P]], -1)
            fill(diagcap[:, :], BIG)
            keep(diagcap[:, :], ALU.is_gt, NEG, 0, [[1, P]], -1)
            fill(newcap[:, :, :], BIG)
            keep(newcap[:, :, :], ALU.is_gt, NEG, 0, [[0, NH], [1, DEC_T]], -1)
            fill(headones[:, :], 0.0)
            fill(headones[0:HD, 0:HD], 1.0)
            fill(headones[HD:P, HD:P], 1.0)
            fill(headrow[:, :], 1.0)
            for r in (0, NH * DEC_T):
                rows = headrow[r:r + NH * DEC_T, :]
                keep(rows, ALU.is_ge, 0.0, 0, [[-DEC_T, NH]], 1)
                keep(rows, ALU.is_ge, 0.0, DEC_T - 1, [[DEC_T, NH]], -1)
            ch.did(pool.memset(zero[:, :], 0.0))
            ch.did(pool.memset(eps[:, :], EPS))
            ch.sync()
            pool.sem_inc(S["consts"], 1)

            unit = [0]

            def stream(phase, per, groups, first_free):
                g, _, _, trips, pattern = PHASES[phase]
                gpi = len(pattern)
                pool.wait_ge(S["products"], first_free)
                ends = np.cumsum(groups).tolist()
                assert ends[-1] == gpi
                with pool.Fori(0, trips) as i:
                    ch.enter(i, per)
                    for u in range(per):
                        prev = ends[u - 2] if u >= 2 else ends[per + u - 2] - gpi
                        pool.wait_ge(S["products"], i * gpi + (g + prev))
                        pool.wait_ge(w_in(u % 2), i * (32 * per // 2) + ((unit[0] + u) // 2 + 1) * 32)
                        ch.did(pool.tensor_tensor(wh[u % 2][:, :], raw[u % 2][:, :], zero[:, 0:1].to_broadcast([P, 2048]), ALU.add))
                        ch.sync()
                        pool.tensor_tensor(wl[u % 2][:, :], raw[u % 2][:, :], wh[u % 2][:, :].bitcast(F32),
                                           ALU.subtract).then_inc(S["split"], 1)
                    ch.leave(trips)
                unit[0] += trips * per

            stream("ada", 2, [1, 1], 1)
            stream("qk", 2, [6, 6], PHASES["qk"][0] - 1)
            stream("v", 2, [9, 9], PHASES["v"][0] - 6)
            stream("conv", 2, [6, 6], PHASES["conv"][0] - 9)
            stream("gates", 2, [6, 6], PHASES["gates"][0] - 6)
            def prompt_steps(p, first=False, last=False):
                for u in range(NSTEP if not last else LATE_PROB):
                    k = u - LATE_SOFTPLUS
                    if (k >= 0 or not first) and (k < 0 or not last):
                        n = 512 - step_of(k)[3]
                        pool.wait_ge(S["sp_hi"], NSTEP * p + (k + 1))
                        pool.tensor_tensor(sl[k % 4][:, 0:n], sp_[k % 3][:, 0:n], sh[k % 4][:, 0:n].bitcast(F32),
                                           ALU.subtract).then_inc(S["sp_lo"], 1)
                    k = u - LATE_PROB
                    if (k >= 0 or not first) and (k < 0 or not last):
                        n = 512 - step_of(k)[3]
                        pool.wait_ge(S["prob_hi"], NSTEP * p + (k + 1))
                        pool.tensor_tensor(pl[k % 3][:, 0:n], prob[k % 3][:, 0:n], ph[k % 3][:, 0:n].bitcast(F32),
                                           ALU.subtract).then_inc(S["prob_lo"], 1)

            prompt_steps(0, first=True)
            with pool.Fori(1, NPAIR) as p:
                prompt_steps(p)
            prompt_steps(NPAIR, last=True)
            with pool.Fori(0, DEC_B) as b:
                for c in range(4):
                    pool.wait_ge(S["v_hi"], 4 * b + (c + 1))
                    pool.tensor_tensor(vl[c][:, :], raw[c % 2][:, :], vh[c][:, :].bitcast(F32), ALU.subtract)\
                        .then_inc(S["v_lo"], 1)
                pool.wait_ge(S["vnew_hi"], b + 1)
                pool.tensor_tensor(vnewL[:, :], vnew[:, :], vnewH[:, :].bitcast(F32), ALU.subtract)\
                    .then_inc(S["vnew_lo"], 1)
            pool.wait_ge(S["d_av"], 5 * DEC_B + CREDIT4)
            stream("mix", 2, [12, 12], PHASES["mix"][0] - 6)
            stream("wo", 2, [6, 6], PHASES["wo"][0] - 12)
            stream("mlp", 4, [6, 6, 12, 12], PHASES["mlp"][0] - 6)

        @block.tensor
        def _(pe):
            for n in ("products",):
                pe.sem_inc(S[n], CREDIT)
            for n in ("z_done", "kt_done", "dz_done", "square_sum", "qk_sum", "ada_sel", "ds_done", "d_otr"):
                pe.sem_inc(S[n], CREDIT)
            pe.sem_inc(S["av_done"], AV_CREDIT)
            for n in ("d_av", "z_used"):
                pe.sem_inc(S[n], CREDIT4)
            unit = [0]

            def three(out, pairs):
                n, last = 0, 3 * len(pairs) - 1
                for lh, ll, rh, rl in pairs:
                    for x, y in ((lh, rh), (lh, rl), (ll, rh)):
                        mm = pe.matmul(out, x, y, start=n == 0, stop=n == last)
                        n += 1
                return mm

            def phase(name, per, body):
                g, vd, va, trips, pattern = PHASES[name]
                pe.wait_ge(S["bank_dve"], vd)
                pe.wait_ge(S["bank_act"], va)
                per_engine = {"d": (S["bank_dve"], vd, pattern.count("d")), "a": (S["bank_act"], va, pattern.count("a"))}

                def emptied(k, i):
                    kk = (k - 2) % len(pattern)
                    s_, base_, cnt = per_engine[pattern[kk]]
                    at = base_ + pattern[:kk + 1].count(pattern[kk]) - (cnt if k < 2 else 0)
                    pe.wait_ge(s_, i * cnt + at)

                def iteration(i):
                    k = 0
                    for u in range(per):
                        pe.wait_ge(S["split"], i * per + (unit[0] + u + 1))
                        for out, pairs in body(i, u):
                            emptied(k, i)
                            three(out(bank[LIN[k % 2]]), pairs).then_inc(S["products"], 1)
                            k += 1
                    assert k == len(pattern), (name, k)

                if trips == 1:
                    iteration(0)
                else:
                    with pe.Fori(0, trips) as i:
                        iteration(i)
                unit[0] += trips * per

            def chunk(c):
                return slice(c * CH, (c + 1) * CH)

            def dense(s, m, c, rh, rl, kts=range(8), width=UC, r0=0):
                return (lambda bk: bk[:, 0:CH],
                        [(wh[s][:, kt * width + m * P:kt * width + m * P + P],
                          wl[s][:, kt * width + m * P:kt * width + m * P + P],
                          rh[:, kt - r0, chunk(c)], rl[:, kt - r0, chunk(c)]) for kt in kts])

            pe.wait_ge(S["consts"], 1)
            pe.wait_ge(S["small_in"], 16 * N_SMALL)
            pe.transpose(bank[0][:, 0:82], vecrow[:, :], ident[0:82, 0:82])
            for c in range(CB):
                mm = pe.transpose(bank[0][:, 96 + 16 * c:112 + 16 * c], histrow[:, c * P:(c + 1) * P], ident[0:16, 0:16])
            mm.then_inc(S["vec_turned"], 1)
            pe.wait_ge(S["c_ready"], 1)
            for kt in range(DB):
                mm = pe.transpose(bank[1][:, 9 * kt:9 * kt + 9], crow[:, kt * P:(kt + 1) * P], ident[0:9, 0:9])
            mm.then_inc(S["c_turned"], 1)
            pe.wait_ge(S["x_in"], 32)
            for t in range(9):
                rows = P if t < 8 else NS
                for half in (0, 1):
                    if t >= 2:
                        pe.wait_ge(S["xT_dve" if half else "xT_act"], t - 1)
                    for b in range(4):
                        mm = pe.transpose(bank[2 + 2 * (t % 2) + half][:, b * P:b * P + rows],
                                          xload[0:rows, t, (4 * half + b) * P:(4 * half + b + 1) * P],
                                          ident[0:rows, 0:rows])
                    mm.then_inc(S["x_turned"], 1)
            g, vd, va, trips, _ = PHASES["ada"]
            pe.wait_ge(S["c_split"], 1)
            pe.wait_ge(S["xT_act"], 9)
            pe.wait_ge(S["xT_dve"], 9)
            with pe.Fori(0, trips) as i:
                for u in (0, 1):
                    pe.wait_ge(S["split"], i * 2 + (u + 1))
                    pe.wait_ge(S["bank_dve"], i * 2 + (vd - 2 + u + 1))
                    out = bank[LIN[u]][0:18, 0:UC]
                    for kt in range(DB):
                        for n, w in enumerate((wh[u], wl[u])):
                            mm = pe.matmul(out, chl[:, kt, :], w[:, kt * UC:(kt + 1) * UC],
                                           start=kt == 0 and n == 0, stop=kt == DB - 1 and n == 1)
                    mm.then_inc(S["products"], 1)
                for u in (0, 1):
                    pe.wait_ge(S["bank_dve"], i * 2 + (vd + u + 1))
                    pe.wait_ge(S["mods_in"], i * 2 + (CREDIT - 2 + u + 1))
                    for m in (0, 1):
                        mm = pe.matmul(bank[2 + u][:, 9 * m:9 * m + 9], adaY[u][:, m * P:(m + 1) * P], sel9[:, :],
                                       start=m == 0, stop=m == 1, skip_group_check=True)
                    mm.then_inc(S["ada_sel"], 1)
            unit[0] = 2 * trips

            def norm_sums(src, n0):
                with pe.Fori(0, NCH) as c:
                    pe.wait_ge(S["mean_read"], c + (CREDIT + n0 // 8))
                    for b in range(DB):
                        pe.wait_ge(S["squares"], c * 8 + (n0 + b + 1))
                        pe.matmul(bank[0][:, 0:CH], ones[:, :], src[b % 2][:, :], start=b == 0,
                                  stop=b == DB - 1).then_inc(S["square_sum"], 1)

            norm_sums(sq, 0)
            pe.wait_ge(S["h_lo"], 8)
            phase("qk", 2, lambda i, u: [dense(u, m, c, hH, hL) for m in (0, 1) for c in range(NCH)])

            def v_groups(i, u):
                for t in range(9):
                    n = P if t < 8 else NS
                    yield (lambda bk, n=n: bk[0:n, 0:UC],
                           [(hH[:, kt, t * P:t * P + n], hL[:, kt, t * P:t * P + n],
                             wh[u][:, kt * UC:(kt + 1) * UC], wl[u][:, kt * UC:(kt + 1) * UC]) for kt in range(DB)])

            phase("v", 2, v_groups)
            with pe.Fori(0, 4) as i:
                for u in (0, 1):
                    pe.wait_ge(S["qk_square"], i * 2 + (u + 1))
                    pe.wait_ge(S["qk_rstd"], i * 2 + (CREDIT - 2 + u + 1))
                    for c in range(NCH):
                        mm = pe.matmul(bank[3 * u + c][:, 0:CH], headones[:, :], qsq[u][:, chunk(c)], start=True, stop=True)
                    mm.then_inc(S["qk_sum"], 1)
            pe.wait_ge(S["qk_ready"], 8 + CREDIT)
            for t in range(9):
                n = P if t < 8 else NS
                if t >= 2:
                    pe.wait_ge(S["kout_ready"], t - 1)
                for b in range(4):
                    mm = pe.transpose(bank[t % 2][0:n, b * P:(b + 1) * P], act8[:, 4 + b, t * P:t * P + n], ident[:, :])
                mm.then_inc(S["kturned"], 1)
            phase("conv", 2, lambda i, u: [dense(u, m, c, hH, hL) for m in (0, 1) for c in range(NCH)])
            phase("gates", 2, lambda i, u: [dense(u, m, c, hH, hL) for m in (0, 1) for c in range(NCH)])
            pe.wait_ge(S["yc_ready"], CB)
            for c in range(CB):
                mm = pe.transpose(bank[0][0:18, c * P:(c + 1) * P], tail[:, c, :], ident[:, :])
            mm.then_inc(S["tail_turned"], 1)

            def scores(p, u):
                qc, j, h, lo, _ = step_of(u)
                rows, keys, qs = slice(HD * h, HD * h + HD), slice(j * P, j * P + P), slice(512 * qc + lo, 512 * qc + 512)
                if u == 0:
                    pe.wait_ge(S["pair_ready"], p + 1)
                pe.wait_ge(S["zb_done"], NSTEP * p + (u - 3 + CREDIT4))
                three(bank[(0, 1, 6, 7)[u % 4]][:, 0:512 - lo], [(kh[rows, keys], kl[rows, keys], qh[rows, qs], ql[rows, qs])])\
                    .then_inc(S["z_done"], 1)

            def block_sums(p, k):
                qc, j, h, lo, _ = step_of(k)
                pe.wait_ge(S["sp_lo"], NSTEP * p + (k + 1))
                if j == 4 * qc + 3:
                    pe.wait_ge(S["arg_done"], NSTEP * p + (k - 1 + CREDIT))
                out = bank[2 + h][:, lo:512]
                n = 512 - lo
                pe.matmul(out, suffix_r[:, :], sh[k % 4][:, 0:n], start=j == 4 * qc + 3, stop=False, skip_group_check=True)
                pe.matmul(out, suffix_r[:, :], sl[k % 4][:, 0:n], start=False, stop=j == 0,
                          skip_group_check=True).then_inc(S["tri_done"], 1)

            def rest_of_block(p, k):
                qc, j, h, lo, _ = step_of(k)
                if j == 0:
                    return
                out = bank[2 + h][:, lo:512]
                pe.wait_ge(S["arg_done"], NSTEP * p + (k + 1 + CREDIT))
                for x in (sh, sl):
                    pe.matmul(out, prefix_r[:, :], x[k % 4][:, 0:512 - lo], start=False, stop=False, skip_group_check=True)

            def values(p, k):
                qc, j, h, lo, _ = step_of(k)
                first = j == 4 * qc + 3
                n = 512 - lo
                if k == 0:
                    pe.wait_ge(S["values_ready"], p + 1)
                pe.wait_ge(S["prob_lo"], NSTEP * p + (k + 1))
                if first:
                    pe.wait_ge(S["o_out"], 4 * p + (4 * (k // NSTEP) + 2 * qc + h - 1 + CREDIT))
                out = bank[4 + h][0:HD, lo:512]
                vH_, vL_ = (v[:, j, HD * h:HD * h + HD] for v in (vcH, vcL))
                pe.matmul(out, vH_, ph[k % 3][:, 0:n], start=first, stop=False, skip_group_check=True)
                pe.matmul(out, vL_, ph[k % 3][:, 0:n], start=False, stop=False, skip_group_check=True)
                pe.matmul(out, vH_, pl[k % 3][:, 0:n], start=False, stop=j == 0, skip_group_check=True)\
                    .then_inc(S["av_done"], 1)

            def prompt_steps(p, first=False, last=False):
                for u in range(NSTEP if not last else LATE_VALUES):
                    if u and not last:
                        scores(p, u)
                    for stage, late in ((block_sums, LATE_SUMS), (rest_of_block, LATE_REST), (values, LATE_VALUES)):
                        k = u - late
                        if (k >= 0 or not first) and (k < 0 or not last):
                            stage(p, k)
                    if u == 0 and not last:
                        scores(p, u)

            pe.wait_ge(S["tail_ready"], 1)
            pe.wait_ge(S["bank_act"], PHASES["mix"][2])
            prompt_steps(0, first=True)
            with pe.Fori(1, NPAIR) as p:
                prompt_steps(p)
            prompt_steps(NPAIR, last=True)

            def turn(b, n):
                c, pr = n // 4, n % 4
                if pr == 0:
                    pe.wait_ge(S[f"k_in{c}"], 64 * b + 64)
                pe.wait_ge(S["kt_lo"], 16 * b + (n - 1 + CREDIT))
                for g in range(4):
                    mm = pe.transpose(bank[n % 2][:, g * P:(g + 1) * P], kraw[c][:, g, pr * P:(pr + 1) * P], ident[:, :])
                mm.then_inc(S["kt_done"], 1)

            def score(b, n):
                c, pr = n // 4, n % 4
                pe.wait_ge(S["kt_lo"], 16 * b + (n + 1 + CREDIT))
                if n == 0:
                    pe.wait_ge(S["q_block"], b + 1)
                if pr == 0 and c < 2 and not (isinstance(b, int) and b == 0):
                    pe.wait_ge(S["zrow_ready"], 5 * b)
                if pr == 0 and c >= 2:
                    pe.wait_ge(S["zrow_ready"], 5 * b + (c - 1))
                out = bank[4 + c % 2][0:ROWS, :]
                qh_, ql_ = (q[:, pr * ROWS:(pr + 1) * ROWS] for q in (qbh, qbl))
                pe.matmul(out, qh_, kTh[:, pr, :], start=pr == 0, stop=False)
                pe.matmul(out, ql_, kTh[:, pr, :], start=False, stop=False)
                pe.matmul(out, qh_, kTl[:, pr, :], start=False, stop=pr == 3).then_inc(S["z_used"], 1)

            def score_new(b):
                pe.wait_ge(S["darg"], b + CREDIT)
                out = bank[3][0:ROWS, 128:128 + DEC_T]
                for pr in range(4):
                    qh_, ql_ = (q[:, pr * ROWS:(pr + 1) * ROWS] for q in (qbh, qbl))
                    pe.matmul(out, qh_, knh[:, pr, :], start=pr == 0, stop=False)
                    pe.matmul(out, ql_, knh[:, pr, :], start=False, stop=False)
                    mm = pe.matmul(out, qh_, knl[:, pr, :], start=False, stop=pr == 3)
                mm.then_inc(S["znew_done"], 1)

            def before_keys_down(b, c):
                pe.wait_ge(S["zrow_ready"], 5 * b + (c + 1 + (c == 3)))
                if c == 0:
                    pe.wait_ge(S["dabs"], b + CREDIT)

            def keys_down(b, c):
                for g in range(4):
                    page = 4 * c + g
                    mm = pe.transpose(bank[6][:, page * ROWS:(page + 1) * ROWS], zrow[:, g * P:(g + 1) * P],
                                      ident[0:ROWS, 0:ROWS])
                if c == 3:
                    mm = pe.transpose(bank[3][0:DEC_T, 64:64 + ROWS], zrow_new[:, :], ident[0:ROWS, 0:ROWS])
                mm.then_inc(S["dz_done"], 1)

            def suffix_sums(b):
                pe.wait_ge(S["dsum_ready"], b + 1)
                pe.wait_ge(S["darg"], b + CREDIT)
                if not (isinstance(b, int) and b == 0):
                    pe.wait_ge(S["d_oout"], b + CREDIT)
                o16, onew = bank[7][:, :], bank[3][:, 96:96 + ROWS]
                pe.matmul(onew, suffix_r[:, :], dsh[:, PAGES, :], start=True, stop=False)
                pe.matmul(onew, suffix_r[:, :], dsl[:, PAGES, :], start=False, stop=True)
                ops = ((suffix_r, dsh), (suffix_r, dsl), (ones_r, dch), (ones_r, dcl))
                for n, (w, r) in enumerate(ops):
                    mm = pe.matmul(o16, w[:, :], r[:, 0:PAGES, :].rearrange("p g c -> p (g c)"), start=n == 0, stop=n == 3)
                mm.then_inc(S["ds_done"], 1)

            def weigh_values(b, before_last=lambda: None):
                pe.wait_ge(S["dprob_lo"], b + 1)
                pe.wait_ge(S["d_osel"], b + CREDIT)
                for c in range(4):
                    pe.wait_ge(S["v_lo"], 4 * b + (c + 1))
                    if c == 3:
                        pe.wait_ge(S["vnew_lo"], b + 1)
                        before_last()
                    for g in range(4):
                        page = 4 * c + g
                        for v in (vh[c], vl[c]):
                            mm = pe.matmul(bank[2][0:2 * ROWS, :], dp2[:, page, :], v[:, g * ATT:(g + 1) * ATT],
                                           start=page == 0 and v is vh[c], stop=False)
                    mm.then_inc(S["d_av"], 1)
                pe.matmul(bank[2][0:2 * ROWS, :], dp2[0:DEC_T, PAGES, :], vnewH[:, :], start=False, stop=False)
                pe.matmul(bank[2][0:2 * ROWS, :], dp2[0:DEC_T, PAGES, :], vnewL[:, :], start=False, stop=True)\
                    .then_inc(S["d_av"], 1)

            def gather_heads(b):
                pe.wait_ge(S["d_osel"], b + (1 + CREDIT))
                pe.wait_ge(S["d_oout"], b + CREDIT)
                for pr in range(4):
                    mm = pe.matmul(bank[3][:, pr * 4:pr * 4 + 4], osel[:, pr * P:(pr + 1) * P], sel4[:, :],
                                   start=True, stop=True)
                mm.then_inc(S["d_otr"], 1)

            def sequence(b, prev=True, prev2=True):
                for n in range(18):
                    if n in (8, 12, 16):
                        before_keys_down(b, n // 4 - 2)
                    if n < 16:
                        turn(b, n)
                    if n >= 2:
                        score(b, n - 2)
                    if n in (8, 12, 16):
                        keys_down(b, n // 4 - 2)
                    if prev2 and n == 5:
                        gather_heads(b - 2)
                    if prev and n == 12:
                        suffix_sums(b - 1)
                score_new(b)
                if prev:
                    weigh_values(b - 1, lambda: before_keys_down(b, 3))
                else:
                    before_keys_down(b, 3)
                keys_down(b, 3)

            pe.wait_ge(S["o_out"], 4 * NPAIR + CREDIT)
            sequence(0, False, False)
            sequence(1, True, False)
            with pe.Fori(2, DEC_B) as b:
                sequence(b)
            gather_heads(DEC_B - 2)
            suffix_sums(DEC_B - 1)
            weigh_values(DEC_B - 1)
            gather_heads(DEC_B - 1)

            pe.wait_ge(S["oy_lo"], 2)
            pe.wait_ge(S["d_oout"], DEC_B + CREDIT)
            phase("mix", 2, lambda i, u: [dense(u, m, c, *((oH, oL) if part == 0 else (ycH, ycL)),
                                                kts=range(4 * part, 4 * part + 4), r0=4 * part)
                                          for m in (0, 1) for part in (0, 1) for c in range(NCH)])
            pe.wait_ge(S["mix_lo"], 3 * DB + 3 * CREDIT)
            phase("wo", 2, lambda i, u: [dense(u, m, c, mixH, mixL) for m in (0, 1) for c in range(NCH)])
            norm_sums(sq2, 24)
            pe.wait_ge(S["h_lo"], 16)

            def mlp_groups(i, u):
                if u < 2:
                    yield from (dense(u, m, c, h2H, h2L) for m in (0, 1) for c in range(NCH))
                    return
                for c in range(NCH):
                    if u == 2:
                        pe.wait_ge(S["hid_lo"], i * 12 + (10 + c))
                    for m in range(4):
                        yield dense(u % 2, m, c, hidH, hidL, kts=range(4), width=512)

            phase("mlp", 4, mlp_groups)
            pe.wait_ge(S["acc_done"], 1)
            for t in range(9):
                n = P if t < 8 else NS
                for half in (0, 1):
                    if t >= 2:
                        pe.wait_ge(S["y_dve" if half else "y_act"], t - 1)
                    for b in range(4):
                        mm = pe.transpose(bank[2 * (t % 2) + half][0:n, b * P:(b + 1) * P],
                                          x1[:, 4 * half + b, t * P:t * P + n], ident[:, :])
                    mm.then_inc(S["y_turned"], 1)

        @block.scalar
        def _(act):
            for n in ("bank_act", "mods_in", "mean_read", "qk_rstd", "prob_done", "o_out"):
                act.sem_inc(S[n], CREDIT)
            act.sem_inc(S["gate_dma0"], 16)
            act.sem_inc(S["gate_dma1"], 16)
            ch = Chain(act, S["act_step"])
            ev = act.activation

            def products(name, at, i=0):
                g, _, _, _, pattern = PHASES[name]
                act.wait_ge(S["products"], i * len(pattern) + (g + at + 1))

            act.preload_act_table_set("natural_log_exp_and_others")
            act.wait_ge(S["small_in"], 16 * N_SMALL)
            ev(csig[:, :], crow[:, :], ACT.Exp, scale=-1.0).then_inc(S["scaled_act"], 1)
            for t in range(9):
                n = P if t < 8 else NS
                act.wait_ge(S["x_turned"], 2 * t + 1)
                ev(act8[:, 0:4, t * P:t * P + n], bank[2 + 2 * (t % 2)][:, 0:4 * P].rearrange("p (b c) -> p b c", b=4)[:, :, 0:n],
                   ACT.Copy).then_inc(S["xT_act"], 1)
            act.wait_ge(S["xT_dve"], 9)
            act.wait_ge(S["xT_act"], 9)
            act.dma_start(x_dram.rearrange("b p t -> p b t"), act8[:, :, :]).then_inc(S["x_saved"], 16)
            with act.Fori(0, 12) as i:
                for u in (0, 1):
                    act.wait_ge(S["ada_sel"], i * 2 + (u + 1 + CREDIT))
                    ev(mods[:, ds(i * 4 + 2 * u, 2), :], bank[2 + u][:, 0:18].rearrange("p (m c) -> p m c", m=2),
                       ACT.Copy).then_inc(S["mods_in"], 1)

            def norm(src, sqt, rs, nr, hf, hi, sbase, n0):
                with act.Fori(0, NCH) as c:
                    for b in range(DB):
                        act.wait_ge(S["square_sum"], c * 8 + (n0 + b - 1 + CREDIT))
                        ev(sqt[b % 2][:, :], src[:, b, ds(c * CH, CH)], ACT.Square).then_inc(S["squares"], 1)
                    act.wait_ge(S["square_sum"], c * 8 + (n0 + 8 + CREDIT))
                    ev(rs[:, ds(c * CH, CH)], bank[0][:, 0:CH], ACT.Ln, scale=1.0 / D, bias=eps[:, :])\
                        .then_inc(S["mean_read"], 1)
                m0 = n0 // 3
                act.wait_ge(S["mean_read"], 3 * (m0 // 8) + NCH + CREDIT)
                ev(rs[:, :], rs[:, :], ACT.Exp, scale=-0.5).then_inc(S["rstd_ready"], 1)
                with act.Fori(0, 4) as i:
                    for u in (0, 1):
                        b = i * 2 + u
                        act.wait_ge(S["normed"], i * 2 + (m0 + u + 1))
                        ev(hf[u][:, 0:SEQ], nr[u][:, 0:SEQ], ACT.Identity, scale=mods[:, b + (sbase + DB), 0:1],
                           bias=mods[:, b + sbase, 0:1]).then_inc(S["scaled_act"], 1)
                        act.wait_ge(S["scaled_dve"], i * 2 + (m0 + u + 1))
                        act.wait_ge(S["scaled_act"], i * 2 + (m0 + u + 2))
                        ev(hi[:, b, :], hf[u][:, :], ACT.Copy).then_inc(S["h_hi"], 1)

            act.wait_ge(S["mods_ready"], 1)
            norm(act8, sq, rstd, nrm, hF, hH, 0, 0)
            act.wait_ge(S["bank_dve"], PHASES["v"][1])
            act.wait_ge(S["h_lo"], 8)
            with act.Fori(0, 4) as i:
                ch.enter(i, 6)
                for u in (0, 1):
                    act.wait_ge(S["qk_sum"], i * 2 + (CREDIT - 2 + u + 1))
                    ev(qsq[u][:, :], act8[:, i * 2 + u, :], ACT.Square).then_inc(S["qk_square"], 1)
                for u in (0, 1):
                    act.wait_ge(S["qk_sum"], i * 2 + (CREDIT + u + 1))
                    act.wait_ge(S["qk_ready"], i * 2 + (u + 1 - 2 + CREDIT))
                    for c in range(NCH):
                        ch.did(ev(qrs[u][:, c * CH:(c + 1) * CH], bank[3 * u + c][:, 0:CH], ACT.Ln, scale=1.0 / HD,
                                  bias=eps[:, :]))
                    ch.sync()
                    ev(qrs[u][:, :], qrs[u][:, :], ACT.Exp, scale=-0.5).then_inc(S["qk_rstd"], 1)
                ch.leave(4)
            act.wait_ge(S["bank_dve"], PHASES["conv"][1])
            act.dma_start(a["v_prompt"][0, 0].rearrange("(t p) h d -> p t (h d)", p=P), vsb[:, 0:8, :]).then_inc(S["v_out"], 16)
            act.dma_start(a["v_sample"][0].rearrange("b t h d -> (b t) (h d)"), vsb[0:NS, 8, :]).then_inc(S["v_out"], 16)
            kd = (S["kout_dma0"], S["kout_dma1"])
            for t in range(9):
                n = P if t < 8 else NS
                act.wait_ge(S["kturned"], t + 1)
                if t >= 2:
                    act.wait_ge(kd[t % 2], 16 * (t // 2))
                ev(kout[t % 2][0:n, :], bank[t % 2][0:n, :], ACT.Copy).then_inc(S["kout_ready"], 1)
                act.wait_ge(S["kout_ready"], t + 1)
                dst = a["k_prompt"][0, 0, t * P:(t + 1) * P].rearrange("t h d -> t (h d)") if t < 8 else \
                    a["k_sample"][0].rearrange("b t h d -> (b t) (h d)")
                act.dma_start(dst, kout[t % 2][0:n, :]).then_inc(kd[t % 2], 16)
            act.wait_ge(kd[0], 5 * 16)
            act.wait_ge(kd[1], 4 * 16)
            act.sem_inc(S["kout_free"], 1)

            gd = (S["gate_dma0"], S["gate_dma1"])

            def gate(name, i, at, u, stored, ready, block_):
                act.wait_ge(gd[u], stored)
                for c in range(NCH):
                    products(name, at + c, i)
                    inst = ev(gt[u][:, c * CH:(c + 1) * CH], bank[LIN[(at + c) % 2]][:, 0:CH], ACT.Exp, scale=-1.0)
                    inst.then_inc(S["bank_act"], 1)
                act.wait_ge(S["gate_ready"], ready)
                act.dma_start(gate_dram[ds(block_, 1), :, :].rearrange("o p t -> (o p) t"), gt[u][:, :]).then_inc(gd[u], 16)

            with act.Fori(0, CB) as i:
                gate("conv", i, 9, 0, i * 16 + 16, i + 1, i)
            act.wait_ge(S["yc_ready"], CB)
            with act.Fori(0, 3) as i:
                for q in range(4):
                    before = (0 if q % 2 else CB) + q // 2
                    gate("gates", i, 3 * q, q % 2, i * 32 + (16 * before + 16), i * 4 + (CB + q + 1), i * 4 + (CB + q))
            act.wait_ge(S["tail_ready"], 1)
            act.dma_start(a["conv_prompt"][0, 0], tailT[0:2, :]).then_inc(S["tail_dma"], 16)
            act.dma_start(a["conv_sample"][0].rearrange("b j c -> (b j) c"), tailT[2:18, :]).then_inc(S["tail_dma"], 16)
            act.wait_ge(gd[0], 16 * 10 + 16)
            act.wait_ge(gd[1], 16 * 6 + 16)
            act.wait_ge(S["tail_dma"], 32)

            act.wait_ge(S["products"], PHASES["mix"][0])

            def prompt_steps(p, first=False, last=False):
                for u in range(NSTEP if not last else LATE_OUT):
                    now = not last and u
                    if now:
                        logarithm(p, u)
                    for stage, late in ((softplus_hi, LATE_SOFTPLUS), (weights, LATE_PROB), (output, LATE_OUT)):
                        k = u - late
                        if (k >= 0 or not first) and (k < 0 or not last):
                            stage(p, k)
                    if u == 0 and not last:
                        if not first:
                            act.wait_ge(S["z_done"], NSTEP * p + CREDIT)
                        ch.did(ev(qh[:, :], act8[:, p, 0:SEQ], ACT.Copy))
                        ev(kh[:, :], act8[:, p + NPAIR, 0:SEQ], ACT.Copy).then_inc(S["qk_hi"], 1)
                        logarithm(p, u)
                    if u == LATE_VALUES - 1 and not last:
                        if not first:
                            act.wait_ge(S["av_done"], NSTEP * p + AV_CREDIT)
                        ev(vcH, vsb[:, 0:8, ds(p * P, P)], ACT.Copy).then_inc(S["values_hi"], 1)

            def logarithm(p, u):
                t = tl[u % 3][:, 0:512 - step_of(u)[3]]
                act.wait_ge(S["absz"], NSTEP * p + (u + 1))
                ch.did(ev(t, t, ACT.Exp))
                ch.sync()
                ev(t, t, ACT.Ln, bias=1.0).then_inc(S["log_done"], 1)

            def softplus_hi(p, k):
                n = 512 - step_of(k)[3]
                act.wait_ge(S["sp_done"], NSTEP * p + (k + 1))
                act.wait_ge(S["av_done"], NSTEP * p + (k - 5 + AV_CREDIT))
                ev(sh[k % 4][:, 0:n], sp_[k % 3][:, 0:n], ACT.Copy).then_inc(S["sp_hi"], 1)

            def weights(p, k):
                n = 512 - step_of(k)[3]
                act.wait_ge(S["arg_done"], NSTEP * p + (k + 1 + CREDIT))
                act.wait_ge(S["av_done"], NSTEP * p + (k - 2 + AV_CREDIT))
                ev(prob[k % 3][:, 0:n], zb[k % 6][:, 0:n], ACT.Exp).then_inc(S["prob_done"], 1)
                act.wait_ge(S["prob_done"], NSTEP * p + (k + 1 + CREDIT))
                ev(ph[k % 3][:, 0:n], prob[k % 3][:, 0:n], ACT.Copy).then_inc(S["prob_hi"], 1)

            def output(p, k):
                qc, j, h, _, _ = step_of(k)
                if j:
                    return
                act.wait_ge(S["av_done"], NSTEP * p + (k + 1 + AV_CREDIT))
                ev(oF[HD * h:HD * h + HD, p + k // NSTEP, 512 * qc:512 * qc + 512], bank[4 + h][0:HD, :], ACT.Copy)\
                    .then_inc(S["o_out"], 1)

            prompt_steps(0, first=True)
            ch.sync()
            with act.Fori(1, NPAIR) as p:
                ch.enter(p - 1, 1 + NSTEP)
                prompt_steps(p)
                ch.leave(NPAIR - 1)
            prompt_steps(NPAIR, last=True)

            def values_hi(b, c):
                act.wait_ge(S[f"v_in{c % 2}"], 128 * b + 64 * (c // 2 + 1))
                if not (isinstance(b, int) and b == 0):
                    act.wait_ge(S["d_av"], 5 * b + (c + 1 - 5 + CREDIT4))
                ev(vh[c][:, :], raw[c % 2][:, :], ACT.Copy).then_inc(S["v_hi"], 1)

            def zrow_out(b, c):
                act.wait_ge(S["z_used"], 16 * b + (4 * c + 4 + CREDIT4))
                act.wait_ge(S["dz_done"], 4 * b + (c + CREDIT))
                ev(zrow[:, :], bank[4 + c % 2][0:ROWS, :], ACT.Copy).then_inc(S["zrow_ready"], 1)

            def sequence(b, now=True, prev=True):
                for n in range(16):
                    if now:
                        act.wait_ge(S["kt_done"], 16 * b + (n + 1 + CREDIT))
                        act.wait_ge(S["z_used"], 16 * b + (n - 3 + CREDIT4))
                        ev(kTh[:, n % 4, :], bank[n % 2][:, :], ACT.Copy).then_inc(S["kt_hi"], 1)
                    if now and n in (6, 10, 14):
                        zrow_out(b, n // 4 - 1)
                    if not prev:
                        continue
                    if n == 2:
                        act.wait_ge(S["dabs"], b + CREDIT)
                        ch.did(ev(dtl[:, :, :], dtl[:, :, :], ACT.Exp))
                        ch.sync()
                        ev(dtl[:, :, :], dtl[:, :, :], ACT.Ln, bias=1.0).then_inc(S["dlog"], 1)
                    if n in (1, 4, 7, 11):
                        values_hi(b - 1, (1, 4, 7, 11).index(n))
                    if n == 9:
                        act.wait_ge(S["dsp_done"], b)
                        ch.did(ev(dsh[:, :, :], dsp[:, :, :], ACT.Copy))
                        ev(dch[:, :, :], dcar[:, 0:PAGES, :], ACT.Copy).then_inc(S["dsp_hi"], 1)
                    if n == 10:
                        act.wait_ge(S["vnew_in"], 16 * b)
                        ev(vnewH[:, :], vnew[:, :], ACT.Copy).then_inc(S["vnew_hi"], 1)
                    if n == 14:
                        act.wait_ge(S["darg"], b + CREDIT)
                        if not (isinstance(b, int) and b == 1):
                            act.wait_ge(S["d_av"], 5 * b + (CREDIT4 - 5))
                        ch.did(ev(dpr[:, :, :], dpr[:, :, :], ACT.Exp))
                        ch.sync()
                        ev(dp2[:, :, 0:ROWS], dpr[:, :, :], ACT.Copy).then_inc(S["dprob"], 1)
                if now:
                    zrow_out(b, 3)
                    act.wait_ge(S["znew_done"], b + 1)
                    ev(zrow_new[:, :], bank[3][0:ROWS, 128:128 + DEC_T], ACT.Copy).then_inc(S["zrow_ready"], 1)

            sequence(0, prev=False)
            sequence(1)
            ch.sync()
            with act.Fori(2, DEC_B) as b:
                ch.enter(b - 2, 3)
                sequence(b)
                ch.leave(DEC_B - 2)
            sequence(DEC_B, now=False)

            act.wait_ge(S["d_oout"], DEC_B + CREDIT)
            act.wait_ge(S["o_out"], 4 * NPAIR + CREDIT)
            act.wait_ge(S["d_av"], 5 * DEC_B + CREDIT4)
            ev(oH[:, :, :], oF[:, :, :], ACT.Copy).then_inc(S["oy_hi"], 1)
            ev(ycH[:, :, :], yc[:, :, :], ACT.Copy).then_inc(S["oy_hi"], 1)
            act.wait_ge(S["oy_lo"], 2)
            with act.Fori(0, DB // 2) as i:
                for m in (0, 1):
                    for c in range(NCH):
                        act.wait_ge(S["mix_done"], i * 6 + (3 * m + c + 1))
                        ev(mixH[:, i * 2 + m, c * CH:(c + 1) * CH], ga[m][:, c * CH:(c + 1) * CH], ACT.Copy)\
                            .then_inc(S["mix_hi"], 1)
            act.wait_ge(S["products"], PHASES["wo"][0])
            act.dma_start(x1[:, :, :], x_dram.rearrange("b p t -> p b t")).then_inc(S["x_back"], 16)
            act.wait_ge(S["x1_ready"], 1)
            norm(x1, sq2, rstd2, nrm2, hF2, h2H, 3 * DB, 24)
            act.wait_ge(S["h_lo"], 16)
            with act.Fori(0, 8) as i:
                for k in range(13):
                    if k < 12:
                        products("mlp", k, i)
                        act.wait_ge(S["sq_done"], i * 12 + (k - 1 + CREDIT))
                        ev(rel[k % 2][:, :], bank[LIN[k % 2]][:, 0:CH], ACT.Relu).then_inc(S["bank_act"], 1)
                    k2 = k - 1
                    if k2 >= 0:
                        m, c = k2 // 3, k2 % 3
                        act.wait_ge(S["sq_done"], i * 12 + (k2 + 1 + CREDIT))
                        ev(hidH[:, m, c * CH:(c + 1) * CH], rsq[k2 % 2][:, :], ACT.Copy).then_inc(S["hid_hi"], 1)
            for t in range(9):
                n = P if t < 8 else NS
                act.wait_ge(S["y_turned"], 2 * t + 1)
                if t >= 2:
                    act.wait_ge(S[f"y_dma{t % 2}"], 16 * (t // 2))
                ev(yrow[t % 2][0:n, 0:512], bank[2 * (t % 2)][0:n, :], ACT.Copy).then_inc(S["y_act"], 1)

        @block.vector
        def _(dve):
            for n in ("bank_dve", "qk_ready", "arg_done", "kt_lo", "dabs", "darg", "d_osel", "d_oout", "sq_done"):
                dve.sem_inc(S[n], CREDIT)
            dve.sem_inc(S["zb_done"], CREDIT4)
            dve.sem_inc(S["mix_lo"], 3 * CREDIT)
            ch = Chain(dve, S["dve_step"])
            ts, tt, stt, cp = dve.tensor_scalar, dve.tensor_tensor, dve.scalar_tensor_tensor, dve.tensor_copy

            def f(t):
                return t.bitcast(F32)

            def step(inst):
                ch.did(inst)

            def products(name, at, i=0):
                g, _, _, _, pattern = PHASES[name]
                dve.wait_ge(S["products"], i * len(pattern) + (g + at + 1))

            def chunk(c):
                return slice(c * CH, (c + 1) * CH)

            dve.wait_ge(S["consts"], 1)
            step(cp(suffix_r[:, :], sfx_f[:, :]))
            step(cp(prefix_r[:, :], pfx_f[:, :]))
            step(cp(ones_r[:, :], ones[:, :]))
            step(tt(sel9[:, :], ident[0:18, 0:9], ident[0:18, 9:18], ALU.add))
            step(dve.tensor_reduce(sel4[:, :], ident[0:64, 0:64].rearrange("p (h q) -> p q h", q=4), AX.X, ALU.add))
            dve.wait_ge(S["scaled_act"], 1)
            step(ts(csig[:, :], csig[:, :], 1.0, None, ALU.add))
            ch.sync()
            step(dve.reciprocal(csig[:, :], csig[:, :]))
            ch.sync()
            tt(crow[:, :], crow[:, :], csig[:, :], ALU.mult).then_inc(S["c_ready"], 1)
            dve.wait_ge(S["vec_turned"], 1)
            step(cp(vec[:, :], bank[0][:, 0:82]))
            step(cp(hist[:, :, :], bank[0][:, 96:160].rearrange("p (b c) -> p b c", b=CB)))
            ch.sync()
            step(ts(gqk[:, 0:4], vec[:, 80:81].to_broadcast([P, 4]), 1.0 / float(np.sqrt(HD)), None, ALU.mult))
            step(cp(gqk[:, 4:8], vec[:, 81:82].to_broadcast([P, 4])))
            dve.wait_ge(S["c_turned"], 1)
            ct = bank[1][:, 0:72].rearrange("p (k c) -> p k c", k=DB)
            step(cp(chl[:, :, 0:9], ct))
            ch.sync()
            tt(chl[:, :, 9:18], ct, f(chl[:, :, 0:9]), ALU.subtract).then_inc(S["c_split"], 1)
            for t in range(9):
                n = P if t < 8 else NS
                dve.wait_ge(S["x_turned"], 2 * t + 2)
                cp(act8[:, 4:8, t * P:t * P + n], bank[3 + 2 * (t % 2)][:, :].rearrange("p (b c) -> p b c", b=4)[:, :, 0:n])\
                    .then_inc(S["xT_dve"], 1)
            with dve.Fori(0, 12) as i:
                for u in (0, 1):
                    products("ada", u, i)
                    dve.wait_ge(S["ada_sel"], i * 2 + (u - 1 + CREDIT))
                    cp(adaY[u][:, :], bank[LIN[u]][0:18, 0:UC]).then_inc(S["bank_dve"], 1)
            dve.wait_ge(S["mods_in"], NMOD * DB // 2 + CREDIT)
            step(tt(mods[:, :, :], mods[:, :, :], vec[:, 0:48].unsqueeze(2).to_broadcast([P, NMOD * DB, 9]), ALU.add))
            ch.sync()
            for g0, v0 in ((DB, 48), (4 * DB, 56)):
                step(stt(mods[:, g0:g0 + DB, :], mods[:, g0:g0 + DB, :], 1.0,
                         vec[:, v0:v0 + DB].unsqueeze(2).to_broadcast([P, DB, 9]), ALU.add, ALU.mult))
            ch.sync()
            dve.sem_inc(S["mods_ready"], 1)

            def per_sequence(col):
                return mods[:, col, 1:9].rearrange("p (o b) -> p o b", o=1).rearrange("p o b -> p (o b)")\
                    .unsqueeze(2).to_broadcast([P, DEC_B, DEC_T])

            def by_sequence(t):
                return t.rearrange("p (b t) -> p b t", b=DEC_B)

            def norm(src, rs, nr, hf, hi, lo, sbase, m0):
                dve.wait_ge(S["rstd_ready"], m0 // 8 + 1)
                with dve.Fori(0, 4) as i:
                    ch.enter(i, 2)
                    for u in (0, 1):
                        tt(nr[u][:, :], src[:, i * 2 + u, :], rs[:, :], ALU.mult).then_inc(S["normed"], 1)
                    for u in (0, 1):
                        b = i * 2 + u
                        dve.wait_ge(S["normed"], i * 2 + (m0 + u + 1))
                        step(tt(by_sequence(nr[u][:, SEQ:T]), by_sequence(nr[u][:, SEQ:T]), per_sequence(b + (sbase + DB)), ALU.mult))
                        ch.sync()
                        tt(by_sequence(hf[u][:, SEQ:T]), by_sequence(nr[u][:, SEQ:T]), per_sequence(b + sbase), ALU.add)\
                            .then_inc(S["scaled_dve"], 1)
                        dve.wait_ge(S["h_hi"], i * 2 + (m0 + u + 1))
                        tt(lo[:, b, :], hf[u][:, :], f(hi[:, b, :]), ALU.subtract).then_inc(S["h_lo"], 1)
                    ch.leave(4)

            norm(act8, rstd, nrm, hF, hH, hL, 0, 0)

            dve.wait_ge(S["x_saved"], 16)
            with dve.Fori(0, 2) as i:
                for k in range(12):
                    products("qk", k, i)
                    cp(act8[:, i * 4 + k // 3, chunk(k % 3)], bank[LIN[k % 2]][:, 0:CH]).then_inc(S["bank_dve"], 1)
            for k in range(18):
                u, t = k // 9, k % 9
                n = P if t < 8 else NS
                products("v", k)
                cp(vsb[0:n, t, u * UC:(u + 1) * UC], bank[LIN[k % 2]][0:n, 0:UC]).then_inc(S["bank_dve"], 1)
            with dve.Fori(0, 4) as i:
                for u in (0, 1):
                    dve.wait_ge(S["qk_rstd"], i * 2 + (u + 1 + CREDIT))
                    b = i * 2 + u
                    stt(act8[:, b, :], act8[:, b, :], gqk[:, ds(b, 1)], qrs[u][:, :], ALU.mult, ALU.mult)\
                        .then_inc(S["qk_ready"], 1)
            dve.wait_ge(S["kout_free"], 1)
            step(dve.memset(up[:, 0:2], 0.0))
            samp = slice(SEQ, T)
            with dve.Fori(0, CB) as i:
                ch.enter(i, 11)
                for c in range(NCH):
                    products("conv", c, i)
                    cp(hcs[:, chunk(c)], bank[LIN[c % 2]][:, 0:CH]).then_inc(S["bank_dve"], 1)
                step(cp(us[:, :, 0:2], hist[:, ds(i, 1), :].rearrange("p o (b j) -> p (o b) j", j=2)))
                for c in range(NCH):
                    k = 3 + c
                    products("conv", k, i)
                    n = CH if c < 2 else LASTP
                    ps = bank[LIN[k % 2]]
                    if c == 0:
                        dve.wait_ge(S["bank_dve"], i * 9 + (PHASES["conv"][1] + 3))
                    one = tt(up[:, 2 + c * CH:2 + c * CH + n], ps[:, 0:n], hcs[:, c * CH:c * CH + n], ALU.mult)
                    if c == 2:
                        step(one)
                        one = tt(us[:, :, 2:6], by_sequence(ps[:, LASTP:CH]), by_sequence(hcs[:, samp]), ALU.mult)
                    one.then_inc(S["bank_dve"], 1)
                dve.wait_ge(S["bank_dve"], i * 9 + (PHASES["conv"][1] + 6))
                ch.sync()
                wt = [vec[:, ds(i + (64 + 4 * j), 1)] for j in range(3)]
                cb = vec[:, ds(i + 76, 1)]
                yp = yc[:, i, 0:SEQ]
                ysm = yc[:, i, samp].rearrange("p (b t) -> p b t", b=DEC_B)
                step(ts(yp, up[:, 0:SEQ], wt[0], cb, ALU.mult, ALU.add))
                step(ts(ysm, us[:, :, 0:4], wt[0], cb, ALU.mult, ALU.add))
                for j in (1, 2):
                    ch.sync()
                    step(stt(yp, up[:, j:j + SEQ], wt[j], yp, ALU.mult, ALU.add))
                    step(stt(ysm, us[:, :, j:j + 4], wt[j], ysm, ALU.mult, ALU.add))
                step(cp(tail[:, i, 0:2], up[:, SEQ:SEQ + 2]))
                step(cp(tail[:, ds(i, 1), 2:18].rearrange("p o (b j) -> p (o b) j", j=2), us[:, :, 4:6]))
                ch.sync()
                for c in range(NCH):
                    k = 6 + c
                    products("conv", k, i)
                    y = yc[:, i, chunk(c)]
                    tt(y, bank[LIN[k % 2]][:, 0:CH], y, ALU.mult).then_inc(S["bank_dve"], 1)
                dve.wait_ge(S["bank_act"], i * 3 + (PHASES["conv"][2] + 3))
                step(ts(gt[0][:, :], gt[0][:, :], 1.0, None, ALU.add))
                ch.sync()
                dve.reciprocal(gt[0][:, :], gt[0][:, :]).then_inc(S["gate_ready"], 1)
                ch.leave(CB)
            dve.wait_ge(S["bank_dve"], PHASES["gates"][1])
            dve.sem_inc(S["yc_ready"], CB)
            with dve.Fori(0, 3) as i:
                ch.enter(i, 4)
                for q in range(4):
                    u = q % 2
                    dve.wait_ge(S["bank_act"], i * 12 + (PHASES["gates"][2] + 3 * q + 3))
                    step(ts(gt[u][:, :], gt[u][:, :], 1.0, None, ALU.add))
                    ch.sync()
                    dve.reciprocal(gt[u][:, :], gt[u][:, :]).then_inc(S["gate_ready"], 1)
                ch.leave(3)
            dve.wait_ge(S["tail_turned"], 1)
            cp(tailT[:, :], bank[0][0:18, :]).then_inc(S["tail_ready"], 1)

            cp(qks[:, :, :], act8[:, :, SEQ:T]).then_inc(S["q_saved"], 1)

            def biased(p, u):
                qc, j, h, lo, diagonal = step_of(u)
                n = 512 - lo
                b = bias8[:, ds(p * 2 + h, 1)]
                z, o = bank[(0, 1, 6, 7)[u % 4]][:, 0:n], zb[u % 6][:, 0:n]
                dve.wait_ge(S["z_done"], NSTEP * p + (u + 1 + CREDIT))
                if u >= 6 or not isinstance(p, int):
                    dve.wait_ge(S["prob_done"], NSTEP * p + (u - 5 + CREDIT))
                if diagonal:
                    one = stt(o[:, 0:P], z[:, 0:P], b, diagcap[:, :], ALU.add, ALU.min)
                    if n > P:
                        step(one)
                        one = ts(o[:, P:n], z[:, P:n], b, None, ALU.add)
                else:
                    one = ts(o, z, b, None, ALU.add)
                one.then_inc(S["zb_done"], 1)
                dve.wait_ge(S["zb_done"], NSTEP * p + (u + 1 + CREDIT4))
                if u >= 3 or not isinstance(p, int):
                    dve.wait_ge(S["sp_done"], NSTEP * p + (u - 2))
                stt(tl[u % 3][:, 0:n], o, -1.0, o, ALU.mult, ALU.min).then_inc(S["absz"], 1)

            def softplus(p, k):
                n = 512 - step_of(k)[3]
                dve.wait_ge(S["log_done"], NSTEP * p + (k + 1))
                if k >= 3 or not isinstance(p, int):
                    dve.wait_ge(S["sp_lo"], NSTEP * p + (k - 2))
                stt(sp_[k % 3][:, 0:n], zb[k % 6][:, 0:n], 0.0, tl[k % 3][:, 0:n], ALU.max, ALU.add).then_inc(S["sp_done"], 1)

            def log_weight(p, k):
                _, _, h, lo, _ = step_of(k)
                o = zb[k % 6][:, 0:512 - lo]
                dve.wait_ge(S["tri_done"], NSTEP * p + (k + 1))
                tt(o, o, bank[2 + h][:, lo:512], ALU.subtract).then_inc(S["arg_done"], 1)

            def prompt_steps(p, first=False, last=False):
                for u in range(NSTEP if not last else LATE_SUMS):
                    if u and not last:
                        biased(p, u)
                    for stage, late in ((softplus, LATE_SOFTPLUS), (log_weight, LATE_SUMS)):
                        k = u - late
                        if (k >= 0 or not first) and (k < 0 or not last):
                            stage(p, k)
                    if u == 0 and not last:
                        dve.wait_ge(S["qk_hi"], p + 1)
                        step(tt(ql[:, :], act8[:, p, 0:SEQ], f(qh[:, :]), ALU.subtract))
                        tt(kl[:, :], act8[:, p + NPAIR, 0:SEQ], f(kh[:, :]), ALU.subtract).then_inc(S["pair_ready"], 1)
                        biased(p, u)
                    if u == LATE_VALUES - 1 and not last:
                        dve.wait_ge(S["values_hi"], p + 1)
                        tt(vcL, vsb[:, 0:8, ds(p * P, P)], f(vcH), ALU.subtract).then_inc(S["values_ready"], 1)

            prompt_steps(0, first=True)
            ch.sync()
            with dve.Fori(1, NPAIR) as p:
                ch.enter(p - 1, 1 + sum(1 for k in range(NSTEP) if step_of(k)[4] and step_of(k)[3] < 512 - P))
                prompt_steps(p)
                ch.leave(NPAIR - 1)
            prompt_steps(NPAIR, last=True)

            dve.wait_ge(S["v_out"], 32)
            dve.wait_ge(S["av_done"], AV_CREDIT + NPAIR * NSTEP)
            step(dve.memset(dzb[:, PAGES, :], NEG))
            step(dve.memset(qbF[:, :], 0.0))
            step(dve.memset(headmask[:, :, :], 1.0))
            step(cp(bias32[:, :, :], bias8[:, :].unsqueeze(2).to_broadcast([P, NH, DEC_T])))
            ch.sync()
            step(dve.tensor_tensor(headmask[:, :, :], headmask[:, :, :],
                                   headrow[:, :].unsqueeze(2).to_broadcast([2 * ROWS, NH, HD]), ALU.mult))
            ch.sync()

            def q_block(b):
                cols = ds(b * DEC_T, DEC_T)
                if not (isinstance(b, int) and b == 0):
                    dve.wait_ge(S["dz_done"], 4 * b + CREDIT)
                pair = qbF[:, :].rearrange("p (r x) -> p r x", x=40)
                step(cp(pair[0:HD, :, 0:4], qks[0:HD, 0:NPAIR, cols]))
                step(cp(pair[HD:P, :, 4:8], qks[HD:P, 0:NPAIR, cols]))
                step(cp(knh[:, :, :], qks[:, NPAIR:DB, cols]))
                ch.sync()
                step(cp(qbh[:, :], qbF[:, :]))
                step(tt(knl[:, :, :], qks[:, NPAIR:DB, cols], f(knh[:, :, :]), ALU.subtract))
                ch.sync()
                tt(qbl[:, :], qbF[:, :], f(qbh[:, :]), ALU.subtract).then_inc(S["q_block"], 1)

            def biased_scores(b):
                dve.wait_ge(S["dz_done"], 4 * b + (4 + CREDIT))
                b32 = bias32[:, :, :].rearrange("p h q -> p (h q)")
                step(tt(dzb[:, 0:PAGES, :], bank[6][:, :].rearrange("p (g c) -> p g c", g=PAGES),
                        b32.unsqueeze(1).to_broadcast([P, PAGES, ROWS]), ALU.add))
                new = dzb[0:DEC_T, PAGES, :]
                step(tt(new, bank[3][0:DEC_T, 64:64 + ROWS], b32[0:DEC_T, :], ALU.add))
                ch.sync()
                step(tt(new, new, newcap[:, :, :].rearrange("p h q -> p (h q)"), ALU.min))
                ch.sync()
                stt(dtl[:, :, :], dzb[:, :, :], -1.0, dzb[:, :, :], ALU.mult, ALU.min).then_inc(S["dabs"], 1)

            def later_pages(b, part):
                for g in range(PAGES - 1 - 4 * part, PAGES - 5 - 4 * part, -1):
                    ch.sync()
                    one = cp(dcar[:, g, :], dsp[:, PAGES, :]) if g == PAGES - 1 else \
                        tt(dcar[:, g, :], dcar[:, g + 1, :], dsp[:, g + 1, :], ALU.add)
                    if g:
                        step(one)
                    else:
                        one.then_inc(S["dsp_done"], 1)

            def sequence(b, now=True, prev=True, prev2=True):
                for n in range(16):
                    if now:
                        dve.wait_ge(S["kt_hi"], 16 * b + (n + 1))
                        tt(kTl[:, n % 4, :], bank[n % 2][:, :], f(kTh[:, n % 4, :]), ALU.subtract).then_inc(S["kt_lo"], 1)
                        if n == 0:
                            q_block(b)
                    if prev and n == 1:
                        biased_scores(b - 1)
                    if prev2 and n == 3:
                        dve.wait_ge(S["d_av"], 5 * b + (5 - 10 + CREDIT4))
                        tt(osel[:, :], bank[2][0:2 * ROWS, :], headmask[:, :, :].rearrange("p h d -> p (h d)"), ALU.mult)\
                            .then_inc(S["d_osel"], 1)
                    if prev and n == 4:
                        dve.wait_ge(S["dlog"], b)
                        step(stt(dsp[:, :, :], dzb[:, :, :], 0.0, dtl[:, :, :], ALU.max, ALU.add))
                    if prev and 5 <= n < 9:
                        later_pages(b - 1, n - 5)
                    if prev2 and n == 9:
                        dve.wait_ge(S["d_otr"], b + (CREDIT - 1))
                        cp(oF[:, :, ds(b * DEC_T + (SEQ - 2 * DEC_T), DEC_T)],
                           bank[3][:, 0:16].rearrange("p (r q) -> p r q", r=4)).then_inc(S["d_oout"], 1)
                    if prev and n == 10:
                        dve.wait_ge(S["dsp_hi"], b)
                        step(tt(dsl[:, :, :], dsp[:, :, :], f(dsh[:, :, :]), ALU.subtract))
                        tt(dcl[:, :, :], dcar[:, 0:PAGES, :], f(dch[:, :, :]), ALU.subtract).then_inc(S["dsum_ready"], 1)
                    if prev and n == 13:
                        dve.wait_ge(S["ds_done"], b + CREDIT)
                        step(tt(dpr[:, 0:PAGES, :].rearrange("p g c -> p (g c)"),
                                dzb[:, 0:PAGES, :].rearrange("p g c -> p (g c)"), bank[7][:, :], ALU.subtract))
                        tt(dpr[:, PAGES, :], dzb[:, PAGES, :], bank[3][:, 96:96 + ROWS], ALU.subtract).then_inc(S["darg"], 1)
                    if prev and n == 15:
                        dve.wait_ge(S["dprob"], b)
                        tt(dp2[:, :, ROWS:2 * ROWS], dpr[:, :, :], f(dp2[:, :, 0:ROWS]), ALU.subtract)\
                            .then_inc(S["dprob_lo"], 1)

            sequence(0, prev=False, prev2=False)
            sequence(1, prev2=False)
            with dve.Fori(2, DEC_B) as b:
                ch.enter(b - 2, 26)
                sequence(b)
                ch.leave(DEC_B - 2)
            sequence(DEC_B, now=False)
            dve.wait_ge(S["d_av"], 5 * DEC_B + CREDIT4)
            tt(osel[:, :], bank[2][0:2 * ROWS, :], headmask[:, :, :].rearrange("p h d -> p (h d)"), ALU.mult)\
                .then_inc(S["d_osel"], 1)
            dve.wait_ge(S["d_otr"], DEC_B + CREDIT)
            cp(oF[:, :, T - DEC_T:T], bank[3][:, 0:16].rearrange("p (r q) -> p r q", r=4)).then_inc(S["d_oout"], 1)

            dve.wait_ge(S["oy_hi"], 1)
            tt(oL[:, :, :], oF[:, :, :], f(oH[:, :, :]), ALU.subtract).then_inc(S["oy_lo"], 1)
            dve.wait_ge(S["oy_hi"], 2)
            tt(ycL[:, :, :], yc[:, :, :], f(ycH[:, :, :]), ALU.subtract).then_inc(S["oy_lo"], 1)
            with dve.Fori(0, 2) as i:
                for u in (0, 1):
                    for m in (0, 1):
                        b = 2 * u + m
                        dve.wait_ge(S[f"gates_in{m}"], i * 64 + 32 * (u + 1))
                        for part, g_ in ((0, ga[m]), (1, gb[m])):
                            for c in range(NCH):
                                k = 12 * u + 6 * m + 3 * part + c
                                products("mix", k, i)
                                tt(g_[:, chunk(c)], bank[LIN[k % 2]][:, 0:CH], g_[:, chunk(c)], ALU.mult)\
                                    .then_inc(S["bank_dve"], 1)
                        for c in range(NCH):
                            dve.wait_ge(S["bank_dve"], i * 24 + (PHASES["mix"][1] + 12 * u + 6 * m + 4 + c))
                            tt(ga[m][:, chunk(c)], ga[m][:, chunk(c)], gb[m][:, chunk(c)], ALU.add).then_inc(S["mix_done"], 1)
                        for c in range(NCH):
                            dve.wait_ge(S["mix_hi"], i * 12 + (3 * b + c + 1))
                            tt(mixL[:, i * 4 + b, chunk(c)], ga[m][:, chunk(c)], f(mixH[:, i * 4 + b, chunk(c)]), ALU.subtract)\
                                .then_inc(S["mix_lo"], 1)

            def gated_add(col, b, c, k):
                ps = bank[LIN[k % 2]]
                n = CH if c < 2 else LASTP
                x = x1[:, b, c * CH:c * CH + n]
                one = stt(x, ps[:, 0:n], mods[:, col, 0:1], x, ALU.mult, ALU.add)
                if c < 2:
                    one.then_inc(S["bank_dve"], 1)
                    return
                step(one)
                ch.sync()
                tt(by_sequence(smp[0][:, :]), by_sequence(ps[:, LASTP:CH]), per_sequence(col), ALU.mult)\
                    .then_inc(S["bank_dve"], 1)

            def sample_add(b):
                x = x1[:, b, samp]
                step(tt(x, x, smp[0][:, :], ALU.add))

            dve.wait_ge(S["x_back"], 16)
            with dve.Fori(0, 2) as i:
                ch.enter(i, 8)
                for k in range(12):
                    b = i * 4 + k // 3
                    products("wo", k, i)
                    gated_add(b + 2 * DB, b, k % 3, k)
                    if k % 3 == 2:
                        dve.wait_ge(S["bank_dve"], i * 12 + (PHASES["wo"][1] + k + 1))
                        sample_add(b)
                        ch.sync()
                ch.leave(2)
            dve.wait_ge(S["bank_dve"], PHASES["mlp"][1])
            dve.sem_inc(S["x1_ready"], 1)
            norm(x1, rstd2, nrm2, hF2, h2H, h2L, 3 * DB, 8)
            with dve.Fori(0, 8) as i:
                ch.enter(i, 16)
                for k in range(12):
                    m, c = k // 3, k % 3
                    dve.wait_ge(S["bank_act"], i * 12 + (PHASES["mlp"][2] + k + 1))
                    tt(rsq[k % 2][:, :], rel[k % 2][:, :], rel[k % 2][:, :], ALU.mult).then_inc(S["sq_done"], 1)
                    dve.wait_ge(S["hid_hi"], i * 12 + (k + 1))
                    tt(hidL[:, m, chunk(c)], rsq[k % 2][:, :], f(hidH[:, m, chunk(c)]), ALU.subtract).then_inc(S["hid_lo"], 1)
                k = 12
                for u in (0, 1):
                    for c in range(NCH):
                        for m in range(4):
                            b = 4 * u + m
                            products("mlp", k, i)
                            if k == 12:
                                ch.sync()
                            gated_add(5 * DB + b, b, c, k)
                            if c == 2:
                                dve.wait_ge(S["bank_dve"], i * 24 + (PHASES["mlp"][1] + k - 12 + 1))
                                sample_add(b)
                            k += 1
                ch.leave(8)
            ch.sync()
            dve.wait_ge(S["bank_dve"], PHASES["mlp"][1] + 8 * 24)
            dve.sem_inc(S["acc_done"], 1)
            for t in range(9):
                n = P if t < 8 else NS
                dve.wait_ge(S["y_turned"], 2 * t + 2)
                if t >= 2:
                    dve.wait_ge(S[f"y_dma{t % 2}"], 16 * (t // 2))
                cp(yrow[t % 2][0:n, 512:D], bank[2 * (t % 2) + 1][0:n, :]).then_inc(S["y_dve"], 1)


IN_NAMES = ("x_prompt x_sample c_prompt c_sample cache_k cache_v state_conv page_table rms_g1 rms_g2 w_ada b_ada w_in "
            "q_norm_g k_norm_g sb_bias conv_w conv_b w_att_out w_conv_out w_o w_mlp1 w_mlp2").split()
OUTS = {
    "y_prompt": (1, SEQ, D), "y_sample": (DEC_B, DEC_T, D),
    "k_prompt": (1, 1, SEQ, NH, HD), "v_prompt": (1, 1, SEQ, NH, HD), "conv_prompt": (1, 1, 2, CONV),
    "k_sample": (1, DEC_B, DEC_T, NH, HD), "v_sample": (1, DEC_B, DEC_T, NH, HD), "conv_sample": (1, DEC_B, 2, CONV),
}


def kernel(**inputs):
    import concourse.bacc as bacc
    from concourse.bass_utils import run_bass_kernel_spmd

    nc = bacc.Bacc("TRN2", target_bir_lowering=False, num_devices=1)
    arrays, aps = {}, {}
    for name in IN_NAMES:
        arr = np.ascontiguousarray(inputs[name])
        arrays["in_" + name] = arr
        aps[name] = nc.dram_tensor("in_" + name, arr.shape, mybir.dt.from_np(arr.dtype), kind="ExternalInput").ap()
    for name, shape in OUTS.items():
        aps[name] = nc.dram_tensor("out_" + name, shape, F32, kind="ExternalOutput").ap()
    program(nc, aps)
    r = run_bass_kernel_spmd(nc, [arrays], core_ids=[0])
    return tuple(r.results[0]["out_" + name] for name in OUTS)
```

```python
from contextlib import ExitStack

import numpy as np
import concourse.bass as bass
from concourse import mybir

F32 = mybir.dt.float32
F32R = mybir.dt.float32r
I32 = mybir.dt.int32
ALU = mybir.AluOpType
ACT = mybir.ActivationFunctionType
AX = mybir.AxisListType
ds = bass.ds

P = 128
D = 1024
SEQ = 1024
DEC_B = 8
DEC_T = 4
NS = DEC_B * DEC_T
T = SEQ + NS
NCH = 3
CH = T // NCH
LASTP = SEQ - 2 * CH
HD = 64
NH = 8
NPAIR = NH // 2
ATT = NH * HD
CONV = 512
CB = CONV // P
FF = 4096
DB = D // P
PAGES = 16
PAGE = 128
NPHYS = 160
EPS = 1e-6
BIG = 3.0e38
NEG = -1.0e30
UC = 256
NMOD = 6
ADA = NMOD * D // UC
ADA_FIRST = 2 * D // UC
CREDIT = 2
CREDIT4 = 4
GROUPS_CREDIT = 8
N_SMALL = 14


class Chain:

    def __init__(self, eng, sem):
        self.eng, self.sem, self.n, self.i, self.per, self.k = eng, sem, 0, None, 0, 0

    def did(self, inst):
        inst.then_inc(self.sem, 1)
        self.k += 1

    def sync(self):
        at = self.n + self.k
        self.eng.wait_ge(self.sem, at if self.i is None else self.i * self.per + at)

    def enter(self, i, per):
        self.n, self.k, self.i, self.per = self.n + self.k, 0, i, per

    def leave(self, trips):
        assert self.k == self.per, f"a loop of {self.k} steps, declared {self.per}"
        self.n, self.k, self.i = self.n + trips * self.per, 0, None


PHASES = {}


def plan():
    g, vd, va = GROUPS_CREDIT, CREDIT, CREDIT
    for name, trips, pattern in (
        ("qk", 2, "d" * 12),
        ("v", 1, "d" * 18),
        ("conv", 4, "d" * 9 + "aaa"),
        ("gates", 3, "a" * 12),
        ("mix", 2, "d" * 24),
        ("wo", 2, "d" * 12),
        ("mlp", 8, "a" * 12 + "d" * 24),
    ):
        PHASES[name] = (g, vd, va, trips, pattern)
        g += trips * len(pattern)
        vd += trips * pattern.count("d")
        va += trips * pattern.count("a")


plan()


def steps_of_pair():
    return [(qc, j, h) for qc in (0, 1) for j in range(4 * qc + 3, -1, -1) for h in (0, 1)]


STEPS = steps_of_pair()
NSTEP = len(STEPS)
LATE_SOFTPLUS, LATE_SUMS, LATE_REST, LATE_PROB, LATE_VALUES, LATE_OUT = 1, 3, 4, 4, 6, 7
H_PARTS = DB * NCH + 1
FIRST_LATE = STEPS.index((1, 7, 0))
QK_SECOND, V_FIRST, V_SECOND = 2, LATE_VALUES - 1, LATE_VALUES + 1
AV_CREDIT = 8


def step_of(k):
    qc, j, h = STEPS[k % NSTEP]
    return qc, j, h, max(0, P * j - 512 * qc), j >= 4 * qc


def program(nc, a):
    ctx = ExitStack()
    with ctx:
        def sem(name):
            return ctx.enter_context(nc.semaphore(name))

        here = [16512]

        def put(name, shape, dt, at=None):
            size = int(np.prod(shape[1:])) * 4
            if at is None:
                at = here[0]
                here[0] += (size + 63) // 64 * 64
            assert at + size <= 229344, name
            return nc.alloc_sbuf_tensor_at(name, shape, dt, offset=at)

        ident = put("ident", [P, P], F32)
        ones = put("ones", [P, P], F32)
        headones = put("headones", [P, P], F32)
        diagcap = put("diagcap", [P, P], F32)
        suffix_r = put("suffix_r", [P, P], F32R)
        prefix_r = put("prefix_r", [P, P], F32R)
        ones_r = put("ones_r", [P, P], F32R)
        newcap = put("newcap", [DEC_T, NH, DEC_T], F32)
        cT = put("cT", [P, DB, 9], F32)
        sel4 = put("sel4", [2 * NH * DEC_T, DEC_T], F32)
        eps = put("eps", [P, 1], F32)
        zero = put("zero", [P, 1], F32)
        mods = put("mods", [P, NMOD * DB, 9], F32)
        vec = put("vec", [P, 82], F32)
        gqk = put("gqk", [P, 8], F32)
        hist = put("hist", [P, CB, 16], F32)
        bias8 = put("bias8", [P, NH], F32)
        headrow = put("headrow", [2 * NH * DEC_T, NH], F32)
        tail = put("tail", [P, CB, 18], F32)
        pages = put("pages", [1, DEC_B * PAGES], I32)
        qks = put("qks", [P, DB, NS], F32)
        vnew = put("vnew", [DEC_T, ATT], F32)
        raw = [put(f"raw{s}", [P, 2048], F32) for s in (0, 1)]
        wh = [put(f"wh{s}", [P, 2048], F32R) for s in (0, 1)]
        wl = [put(f"wl{s}", [P, 2048], F32R) for s in (0, 1)]
        BLK = T * 4
        base = here[0]

        def blk(name, b, shape, dt, extra=0):
            return put(name, shape, dt, at=base + b * BLK + extra)

        xload = blk("xload", 0, [P, 9, D], F32)
        vecrow = blk("vecrow", 9, [82, P], F32)
        histrow = blk("histrow", 9, [16, CONV], F32, 512)
        crow = blk("crow", 10, [9, D], F32)
        csig = blk("csig", 11, [P, DB, 9], F32)
        sfx_f = blk("sfx_f", 12, [P, P], F32)
        pfx_f = blk("pfx_f", 12, [P, P], F32, 512)
        adaY = [blk(f"adaY{s}", 35, [9, UC], F32, 1024 * s) for s in (0, 1)]
        hH = blk("hH", 0, [P, DB, T], F32R)
        hL = blk("hL", 8, [P, DB, T], F32R)
        act8 = blk("act8", 16, [P, DB, T], F32)
        vsb = blk("vsb", 24, [P, 9, ATT], F32)
        us = blk("us", 24, [P, DEC_B, 6], F32, 18432)
        sq = [blk(f"sq{s}", 29 + s, [P, T], F32) for s in (0, 1)]
        acc = blk("acc", 31, [P, T], F32)
        rstd = blk("rstd", 32, [P, T], F32)
        scaled = [blk(f"scaled{s}", 33, [P, CH], F32, 1408 * s) for s in range(3)]
        hs = blk("hs", 34, [P, DB, NS], F32)
        qsq = [blk(f"qsq{s}", 29 + s, [P, T], F32) for s in (0, 1)]
        qrs = [blk(f"qrs{s}", 31 + s, [P, T], F32) for s in (0, 1)]
        kout = [blk(f"kout{s}", 33 + s, [P, ATT], F32) for s in (0, 1)]
        gt = [blk(f"gt{s}", 29 + s, [P, T], F32) for s in (0, 1)]
        hcs = gt[1]
        up = blk("up", 31, [P, 2 + SEQ], F32)
        yc = blk("yc", 32, [P, CB, T], F32)
        tailT = blk("tailT", 31, [18, CONV], F32)
        kh = blk("kh", 0, [P, SEQ], F32R)
        kl = blk("kl", 0, [P, SEQ], F32R, 4096)
        qh = blk("qh", 0, [P, SEQ], F32R, 8192)
        ql = blk("ql", 0, [P, SEQ], F32R, 12288)
        zb = [blk(f"zb{s}", 0, [P, 512], F32, 16384 + 2048 * s) for s in range(6)]
        tl = [blk(f"tl{s}", 0, [P, 512], F32, 28672 + 2048 * s) for s in range(3)]
        sh = [blk(f"sh{s}", 0, [P, 512], F32R, 34816 + 2048 * s) for s in range(4)]
        prob = [blk(f"prob{s}", 0, [P, 512], F32, 43008 + 2048 * s) for s in range(3)]
        sp_ = [blk(f"sp{s}", 29, [P, 512], F32, 2048 * s) for s in range(3)]
        ph = [blk(f"ph{s}", 29, [P, 512], F32R, 6144 + 2048 * s) for s in range(3)]
        sl = [wh[0][:, 512 * s:512 * s + 512] for s in range(4)]
        pl = [wh[1][:, 512 * s:512 * s + 512] for s in range(3)]
        vcH, vcL = (wl[0][:, at:at + SEQ].rearrange("p (t d) -> p t d", t=8) for at in (0, SEQ))
        oF = blk("oF", 12, [P, NPAIR, T], F32)
        kraw = [blk(f"kraw{s}", 16, [P, 4, ATT], F32, 8192 * s) for s in range(4)]
        vh = [wh[0], wh[1]] + [blk(f"vh{s}", 0, [P, 2048], F32R, 8192 * (s - 2)) for s in (2, 3)]
        vl = [wl[0], wl[1]] + [blk(f"vl{s}", 0, [P, 2048], F32R, 8192 * s) for s in (2, 3)]
        kTh = blk("kTh", 0, [P, 4, 512], F32R, 32768)
        kTl = blk("kTl", 0, [P, 4, 512], F32R, 40960)
        DP = PAGES + 1
        dnext = [0]

        def dec(name, shape, dt):
            size = int(np.prod(shape[1:])) * 4
            t = blk(name, 24, shape, dt, dnext[0])
            dnext[0] += (size + 63) // 64 * 64
            assert dnext[0] <= 8 * BLK
            return t

        ROWS = NH * DEC_T
        dzb = dec("dzb", [P, DP, ROWS], F32)
        dpr = dec("dpr", [P, DP, ROWS], F32)
        dtl = dec("dtl", [P, DP, ROWS], F32)
        dcar = dtl
        dsp = dec("dsp", [P, DP, ROWS], F32)
        dsh = dec("dsh", [P, DP, ROWS], F32R)
        dsl = dec("dsl", [P, DP, ROWS], F32R)
        dch = dec("dch", [P, PAGES, ROWS], F32R)
        dcl = dec("dcl", [P, PAGES, ROWS], F32R)
        dp2 = dec("dp2", [P, DP, 2 * ROWS], F32R)
        headmask = dec("headmask", [2 * ROWS, NH, HD], F32)
        osel = dec("osel", [2 * ROWS, ATT], F32)
        vnewH = dec("vnewH", [DEC_T, ATT], F32R)
        vnewL = dec("vnewL", [DEC_T, ATT], F32R)
        qbF = blk("qbF", 0, [P, 5 * ROWS], F32, 49152)
        qbh = blk("qbh", 0, [P, 5 * ROWS], F32R, 49152 + 640)
        qbl = dec("qbl", [P, 5 * ROWS], F32R)
        zrow = dec("zrow", [ROWS, 512], F32)
        zrow_new = dec("zrow_new", [ROWS, DEC_T], F32)
        knh = dec("knh", [P, NPAIR, DEC_T], F32R)
        knl = dec("knl", [P, NPAIR, DEC_T], F32R)
        bias32 = dec("bias32", [P, NH, DEC_T], F32)
        oH = blk("oH", 16, [P, NPAIR, T], F32R)
        oL = blk("oL", 20, [P, NPAIR, T], F32R)
        ycH = blk("ycH", 24, [P, CB, T], F32R)
        ycL = blk("ycL", 28, [P, CB, T], F32R)
        ga = [blk(f"ga{s}", 32 + 2 * s, [P, T], F32) for s in (0, 1)]
        gb = [blk(f"gb{s}", 33 + 2 * s, [P, T], F32) for s in (0, 1)]
        mixH = blk("mixH", 0, [P, DB, T], F32R)
        mixL = blk("mixL", 8, [P, DB, T], F32R)
        x1 = blk("x1", 24, [P, DB, T], F32)
        h2H = blk("h2H", 0, [P, DB, T], F32R)
        h2L = blk("h2L", 8, [P, DB, T], F32R)
        sq2 = [blk(f"sq2{s}", 16 + s, [P, T], F32) for s in (0, 1)]
        acc2 = blk("acc2", 18, [P, T], F32)
        rstd2 = blk("rstd2", 19, [P, T], F32)
        scaled2 = [blk(f"scaled2{s}", 20, [P, CH], F32, 1408 * s) for s in range(3)]
        hs2 = blk("hs2", 21, [P, DB, NS], F32)
        hidH = blk("hidH", 16, [P, 4, T], F32R)
        hidL = blk("hidL", 20, [P, 4, T], F32R)
        rel = [blk(f"rel{s}", 32, [P, CH], F32, 1408 * s) for s in (0, 1)]
        rsq = [blk(f"rsq{s}", 33, [P, CH], F32, 1408 * s) for s in (0, 1)]
        smp = [blk(f"smp{s}", 34, [P, NS], F32, 128 * s) for s in (0, 1)]
        yrow = blk("yrow", 0, [P, 9, D], F32)

        bank = [ctx.enter_context(nc.psum_tensor(f"bank{b}", [P, 512], F32)) for b in range(8)]
        LIN = (6, 7)

        x_dram = nc.dram_tensor("x_scratch", (DB, P, T), F32).ap()
        gate_dram = nc.dram_tensor("gate_scratch", (16, P, T), F32).ap()

        S = {n: sem(n) for n in """
            small_in x_in raw_in0 raw_in1 consts pool_step split products bank_dve bank_act dve_step act_step
            c_exp c_ready c_turned vec_turned ada_used ada_y ada_turned mods_in mods_ready x_turned xT_act
            xT_dve x_saved squares squares_added squares_summed rstd_ready scaled_ready h_hi h_lo qk_square
            qk_sum qk_rstd qk_ready v_out kturned kout_ready kout_dma0 kout_dma1 kout_free gate_ready gate_dma0
            gate_dma1 yc_ready tail_turned tail_ready tail_dma qk_hi pair_ready values_hi values_ready z_done
            zb_done absz log_done sp_done sp_hi sp_lo tri_done arg_done prob_done prob_hi prob_lo av_done o_out
            q_saved k_in0 k_in1 k_in2 k_in3 v_in0 v_in1 vnew_in v_hi v_lo vnew_hi vnew_lo kt_done kt_hi kt_lo
            z_used znew_done zrow_ready dz_done dabs dlog dsp_done dsp_hi dsum_ready ds_done darg dprob dprob_lo
            d_av q_block d_osel d_otr d_oout oy_hi oy_lo gates_in0 gates_in1 mix_done mix_hi mix_lo x_back
            x1_done sq_done hid_hi hid_lo acc_done y_turned y_act y_dve y_dma
        """.split()}

        def w_in(n):
            return S[f"raw_in{n}"]

        block = ctx.enter_context(nc.Block())

        win = a["w_in"][0].rearrange("(k p) n -> p k n", p=P)
        wada = a["w_ada"][0].rearrange("(k p) n -> p k n", p=P)
        wo = a["w_o"][0].rearrange("(k p) n -> p k n", p=P)
        wao = a["w_att_out"][0].rearrange("(k p) n -> p k n", p=P)
        wco = a["w_conv_out"][0].rearrange("(k p) n -> p k n", p=P)
        w1 = a["w_mlp1"][0].rearrange("(k p) n -> p k n", p=P)
        w2 = a["w_mlp2"][0].rearrange("(g k p) n -> g p k n", k=4, p=P)
        ck = a["cache_k"][0].rearrange("g t h d -> g t (h d)")
        cv = a["cache_v"][0].rearrange("g t h d -> g t (h d)")
        O_HC, O_B, O_C, O_GA = 3 * ATT, 3 * ATT + CONV, 3 * ATT + 2 * CONV, 3 * ATT + 3 * CONV

        @block.sync
        def _(sp):
            unit = [0]

            def load_unit(s, n, halves):
                sp.wait_ge(S["split"], n - 1 + CREDIT)
                for dst, src in halves:
                    sp.dma_start(dst, src).then_inc(w_in(s), 16)

            def cols(s, w, col):
                v = raw[s][:, :].rearrange("p (k n) -> p k n", k=8)
                return [(v[:, 4 * h:4 * h + 4, :], w[:, 4 * h:4 * h + 4, ds(col, UC)]) for h in (0, 1)]

            def two_cols(s, w, col0, col1):
                v = raw[s][:, :].rearrange("p (k n) -> p k n", k=8)
                return [(v[:, :, 0:P], w[:, :, ds(col0, P)]), (v[:, :, P:UC], w[:, :, ds(col1, P)])]

            def stream(trips, per, units):
                with sp.Fori(0, trips) as i:
                    for u in range(per):
                        load_unit(u % 2, i * per + (unit[0] + u), units(i, u))
                unit[0] += trips * per

            small = [
                (vecrow[0:48, :], a["b_ada"][0].rearrange("(r c) -> r c", c=P)),
                (vecrow[48:56, :], a["rms_g1"][0].rearrange("(r c) -> r c", c=P)),
                (vecrow[56:64, :], a["rms_g2"][0].rearrange("(r c) -> r c", c=P)),
                (vecrow[64:76, :], a["conv_w"][0].rearrange("j (r c) -> (j r) c", c=P)),
                (vecrow[76:80, :], a["conv_b"][0].rearrange("(r c) -> r c", c=P)),
                (vecrow[80:81, 0:HD], a["q_norm_g"][0:1, :]),
                (vecrow[80:81, HD:P], a["q_norm_g"][0:1, :]),
                (vecrow[81:82, 0:HD], a["k_norm_g"][0:1, :]),
                (vecrow[81:82, HD:P], a["k_norm_g"][0:1, :]),
                (histrow[:, :], a["state_conv"][0].rearrange("b j c -> (b j) c")),
                (crow[0:1, :], a["c_prompt"]),
                (crow[1:9, :], a["c_sample"]),
                (bias8[:, :], a["sb_bias"][0].partition_broadcast(P)),
                (pages[:, :], a["page_table"].rearrange("(o b) g -> o (b g)", o=1)),
            ]
            for dst, src in small:
                sp.dma_start(dst, src).then_inc(S["small_in"], 16)
            assert len(small) == N_SMALL

            def load_ada(n, col):
                if n >= 2:
                    sp.wait_ge(S["ada_used"], n - 1)
                for dst, src in cols(n % 2, wada, col):
                    sp.dma_start(dst, src).then_inc(w_in(n % 2), 16)

            for n in (0, 1):
                load_ada(n, n * UC)
            sp.dma_start(xload[:, 0:8, :], a["x_prompt"][0].rearrange("(t p) d -> p t d", p=P)).then_inc(S["x_in"], 16)
            sp.dma_start(xload[0:NS, 8, :], a["x_sample"].rearrange("b t d -> (b t) d")).then_inc(S["x_in"], 16)
            for n in range(2, ADA_FIRST):
                load_ada(n, n * UC)
            sp.wait_ge(S["ada_used"], ADA_FIRST)
            stream(2, 2, lambda i, u: cols(u, win, i * (2 * UC) + u * UC))
            stream(1, 2, lambda i, u: cols(u, win, 2 * ATT + u * UC))
            sp.wait_ge(S["split"], unit[0] + CREDIT)
            with sp.Fori(0, (ADA - ADA_FIRST) // 2) as i:
                for u in (0, 1):
                    sp.wait_ge(S["ada_used"], i * 2 + (ADA_FIRST + u - 1))
                    for dst, src in cols(u, wada, i * (2 * UC) + (ADA_FIRST + u) * UC):
                        sp.dma_start(dst, src).then_inc(w_in(u), 16)
            sp.wait_ge(S["ada_used"], ADA)
            stream(4, 2, lambda i, u: two_cols(u, win, i * P + (O_B if u else O_HC), i * P + (O_GA if u else O_C)))
            stream(3, 2, lambda i, u: cols(u, win, i * (2 * UC) + (O_GA + CONV + u * UC)))

            def merge_unit(i, u):
                v = raw[u][:, :].rearrange("p (k n) -> p k n", k=8)
                at = i * (2 * UC) + u * UC
                return [(v[:, 0:4, :], wao[:, :, ds(at, UC)]), (v[:, 4:8, :], wco[:, :, ds(at, UC)])]

            def page_numbers(b, c):
                return nc.values_load_multi_w_load_instructions(
                    pages[0:1, ds(b * PAGES + 4 * c, 4)], engines=(mybir.EngineType.SP,), min_val=0, max_val=NPHYS - 1)[1]

            def load_k(b, c):
                numbers = page_numbers(b, c)
                if not (isinstance(b, int) and b == 0):
                    sp.wait_ge(S["kt_done"], 16 * b + (4 * (c + 1) - 16 + CREDIT))
                for g, page in enumerate(numbers):
                    sp.dma_start(kraw[c][:, g, :], ck[page, :, :]).then_inc(S[f"k_in{c}"], 16)

            def load_v(b, c):
                numbers = page_numbers(b, c)
                if not (isinstance(b, int) and b == 0 and c < 2):
                    sp.wait_ge(S["v_lo"], 4 * b + (c - 1))
                dst = raw[c % 2][:, :].rearrange("p (g c) -> p g c", g=4)
                for g, page in enumerate(numbers):
                    sp.dma_start(dst[:, g, :], cv[page, :, :]).then_inc(S[f"v_in{c % 2}"], 16)

            def load_new_v(b):
                if not (isinstance(b, int) and b == 0):
                    sp.wait_ge(S["vnew_lo"], b)
                sp.dma_start(vnew[:, :], a["v_sample"][0, b].rearrange("t h d -> t (h d)")).then_inc(S["vnew_in"], 16)

            sp.wait_ge(S["split"], unit[0] + CREDIT)
            for c in (0, 1):
                load_v(0, c)
            sp.wait_ge(S["v_out"], 32)
            load_new_v(0)
            sp.wait_ge(S["pair_ready"], 2 * NPAIR)
            sp.wait_ge(S["q_saved"], 1)
            for c in range(4):
                load_k(0, c)
            for c in range(4):
                load_k(1, c)
            with sp.Fori(2, DEC_B) as b:
                load_v(b - 2, 2)
                load_k(b, 0)
                load_v(b - 2, 3)
                load_k(b, 1)
                load_v(b - 1, 0)
                load_k(b, 2)
                load_v(b - 1, 1)
                load_new_v(b - 1)
                load_k(b, 3)
            load_v(DEC_B - 2, 2)
            load_v(DEC_B - 2, 3)
            load_v(DEC_B - 1, 0)
            load_v(DEC_B - 1, 1)
            load_new_v(DEC_B - 1)
            load_v(DEC_B - 1, 2)
            load_v(DEC_B - 1, 3)
            sp.wait_ge(S["v_lo"], 4 * DEC_B)
            for u in (0, 1):
                load_unit(u, unit[0] + u, merge_unit(0, u))

            sp.wait_ge(S["oy_lo"], 2 * NCH)
            sp.wait_ge(S["gate_dma0"], 16 * 10 + 16)
            sp.wait_ge(S["gate_dma1"], 16 * 6 + 16)
            gin = (S["gates_in0"], S["gates_in1"])

            def load_gates(i, u):
                for m in (0, 1):
                    b = i * 4 + (2 * u + m)
                    sp.wait_ge(S["mix_lo"], 12 * i + (3 * (2 * u + m - 1) + 3 * CREDIT))
                    sp.dma_start(ga[m][:, :], gate_dram[ds(b, 1), :, :].rearrange("o p t -> (o p) t")).then_inc(gin[m], 16)
                    sp.dma_start(gb[m][:, :], gate_dram[ds(b + DB, 1), :, :].rearrange("o p t -> (o p) t")).then_inc(gin[m], 16)

            for u in (0, 1):
                load_gates(0, u)
            for u in (0, 1):
                load_unit(u, unit[0] + 2 + u, merge_unit(1, u))
                load_gates(1, u)
            unit[0] += 4
            stream(2, 2, lambda i, u: cols(u, wo, i * (2 * UC) + u * UC))

            def mlp_unit(i, u):
                if u < 2:
                    return cols(u, w1, i * (2 * UC) + u * UC)
                v = raw[u % 2][:, :].rearrange("p (k n) -> p k n", k=4)
                return [(v[:, 2 * h:2 * h + 2, :],
                         w2[ds(i, 1), :, 2 * h:2 * h + 2, (u - 2) * 512:(u - 1) * 512].rearrange("o p k n -> (o p) k n"))
                        for h in (0, 1)]

            stream(8, 4, mlp_unit)

            for t in range(9):
                sp.wait_ge(S["y_act"], t + 1)
                sp.wait_ge(S["y_dve"], t + 1)
                if t < 8:
                    sp.dma_start(a["y_prompt"][0, t * P:(t + 1) * P, :], yrow[:, t, :]).then_inc(S["y_dma"], 16)
                else:
                    sp.dma_start(a["y_sample"].rearrange("b t d -> (b t) d"), yrow[0:NS, t, :]).then_inc(S["y_dma"], 16)
            sp.wait_ge(S["y_dma"], 9 * 16)
            sp.wait_ge(S["kout_dma0"], 5 * 16)
            sp.wait_ge(S["kout_dma1"], 4 * 16)
            sp.wait_ge(S["v_out"], 2 * 16)
            sp.wait_ge(S["tail_dma"], 2 * 16)
            sp.wait_ge(S["x_saved"], 16)

        @block.gpsimd
        def _(pool):
            pool.sem_inc(S["split"], CREDIT)
            ch = Chain(pool, S["pool_step"])

            def fill(t, value):
                ch.did(pool.memset(t, value))
                ch.sync()

            def keep(t, cmp, fillv, base_, pattern, cm):
                ch.did(pool.affine_select(out=t, in_=t, compare_op=cmp, fill=fillv, base=base_, pattern=pattern,
                                          channel_multiplier=cm))
                ch.sync()

            fill(ident[:, :], 0.0)
            keep(ident[:, :], ALU.not_equal, 1.0, 0, [[-1, P]], 1)
            fill(ones[:, :], 1.0)
            fill(sfx_f[:, :], 1.0)
            keep(sfx_f[:, :], ALU.is_ge, 0.0, 0, [[-1, P]], 1)
            fill(pfx_f[:, :], 1.0)
            keep(pfx_f[:, :], ALU.is_gt, 0.0, 0, [[1, P]], -1)
            fill(diagcap[:, :], BIG)
            keep(diagcap[:, :], ALU.is_gt, NEG, 0, [[1, P]], -1)
            fill(newcap[:, :, :], BIG)
            keep(newcap[:, :, :], ALU.is_gt, NEG, 0, [[0, NH], [1, DEC_T]], -1)
            fill(headones[:, :], 0.0)
            fill(headones[0:HD, 0:HD], 1.0)
            fill(headones[HD:P, HD:P], 1.0)
            fill(headrow[:, :], 1.0)
            for r in (0, NH * DEC_T):
                rows = headrow[r:r + NH * DEC_T, :]
                keep(rows, ALU.is_ge, 0.0, 0, [[-DEC_T, NH]], 1)
                keep(rows, ALU.is_ge, 0.0, DEC_T - 1, [[DEC_T, NH]], -1)
            ch.did(pool.memset(zero[:, :], 0.0))
            ch.did(pool.memset(eps[:, :], EPS))
            ch.sync()
            pool.sem_inc(S["consts"], 1)

            unit = [ADA_FIRST]

            def stream(phase, per, groups, first_free):
                g, _, _, trips, pattern = PHASES[phase]
                gpi = len(pattern)
                pool.wait_ge(S["products"], first_free)
                ends = np.cumsum(groups).tolist()
                assert ends[-1] == gpi
                with pool.Fori(0, trips) as i:
                    ch.enter(i, per)
                    for u in range(per):
                        prev = ends[u - 2] if u >= 2 else ends[per + u - 2] - gpi
                        pool.wait_ge(S["products"], i * gpi + (g + prev))
                        pool.wait_ge(w_in(u % 2), i * (32 * per // 2) + ((unit[0] + u) // 2 + 1) * 32)
                        ch.did(pool.tensor_tensor(wh[u % 2][:, :], raw[u % 2][:, :], zero[:, 0:1].to_broadcast([P, 2048]), ALU.add))
                        ch.sync()
                        pool.tensor_tensor(wl[u % 2][:, :], raw[u % 2][:, :], wh[u % 2][:, :].bitcast(F32),
                                           ALU.subtract).then_inc(S["split"], 1)
                    ch.leave(trips)
                unit[0] += trips * per

            stream("qk", 2, [6, 6], PHASES["qk"][0] - 1)
            stream("v", 2, [9, 9], PHASES["v"][0] - 6)
            unit[0] += ADA - ADA_FIRST
            stream("conv", 2, [6, 6], PHASES["conv"][0] - 9)
            stream("gates", 2, [6, 6], PHASES["gates"][0] - 6)
            def prompt_steps(p, first=False, last=False):
                for u in range(NSTEP if not last else LATE_PROB):
                    k = u - LATE_SOFTPLUS
                    if (k >= 0 or not first) and (k < 0 or not last):
                        n = 512 - step_of(k)[3]
                        pool.wait_ge(S["sp_hi"], NSTEP * p + (k + 1))
                        pool.tensor_tensor(sl[k % 4][:, 0:n], sp_[k % 3][:, 0:n], sh[k % 4][:, 0:n].bitcast(F32),
                                           ALU.subtract).then_inc(S["sp_lo"], 1)
                    k = u - LATE_PROB
                    if (k >= 0 or not first) and (k < 0 or not last):
                        n = 512 - step_of(k)[3]
                        pool.wait_ge(S["prob_hi"], NSTEP * p + (k + 1))
                        pool.tensor_tensor(pl[k % 3][:, 0:n], prob[k % 3][:, 0:n], ph[k % 3][:, 0:n].bitcast(F32),
                                           ALU.subtract).then_inc(S["prob_lo"], 1)

            prompt_steps(0, first=True)
            with pool.Fori(1, NPAIR) as p:
                prompt_steps(p)
            prompt_steps(NPAIR, last=True)
            with pool.Fori(0, DEC_B) as b:
                for c in range(4):
                    pool.wait_ge(S["v_hi"], 8 * b + 2 * (c + 1))
                    pool.tensor_tensor(vl[c][:, :], raw[c % 2][:, :], vh[c][:, :].bitcast(F32), ALU.subtract)\
                        .then_inc(S["v_lo"], 1)
                pool.wait_ge(S["vnew_hi"], b + 1)
                pool.tensor_tensor(vnewL[:, :], vnew[:, :], vnewH[:, :].bitcast(F32), ALU.subtract)\
                    .then_inc(S["vnew_lo"], 1)
            pool.wait_ge(S["d_av"], 5 * DEC_B + CREDIT4)
            stream("mix", 2, [12, 12], PHASES["mix"][0] - 6)
            stream("wo", 2, [6, 6], PHASES["wo"][0] - 12)
            stream("mlp", 4, [6, 6, 12, 12], PHASES["mlp"][0] - 6)

        @block.tensor
        def _(pe):
            pe.sem_inc(S["products"], GROUPS_CREDIT)
            for n in ("z_done", "kt_done", "dz_done", "qk_sum", "ada_turned", "ds_done", "d_otr"):
                pe.sem_inc(S[n], CREDIT)
            pe.sem_inc(S["av_done"], AV_CREDIT)
            for n in ("d_av", "z_used"):
                pe.sem_inc(S[n], CREDIT4)
            unit = [0]

            def three(out, pairs):
                n, last = 0, 3 * len(pairs) - 1
                for lh, ll, rh, rl in pairs:
                    for x, y in ((lh, rh), (lh, rl), (ll, rh)):
                        mm = pe.matmul(out, x, y, start=n == 0, stop=n == last)
                        n += 1
                return mm

            def phase(name, per, body):
                g, vd, va, trips, pattern = PHASES[name]
                pe.wait_ge(S["bank_dve"], vd)
                pe.wait_ge(S["bank_act"], va)
                per_engine = {"d": (S["bank_dve"], vd, pattern.count("d")), "a": (S["bank_act"], va, pattern.count("a"))}

                def emptied(k, i):
                    kk = (k - 2) % len(pattern)
                    s_, base_, cnt = per_engine[pattern[kk]]
                    at = base_ + pattern[:kk + 1].count(pattern[kk]) - (cnt if k < 2 else 0)
                    pe.wait_ge(s_, i * cnt + at)

                def iteration(i):
                    k = 0
                    for u in range(per):
                        pe.wait_ge(S["split"], i * per + (unit[0] + u + 1 + CREDIT))
                        for out, pairs in body(i, u):
                            emptied(k, i)
                            three(out(bank[LIN[k % 2]]), pairs).then_inc(S["products"], 1)
                            k += 1
                    assert k == len(pattern), (name, k)

                if trips == 1:
                    iteration(0)
                else:
                    with pe.Fori(0, trips) as i:
                        iteration(i)
                unit[0] += trips * per

            def chunk(c):
                return slice(c * CH, (c + 1) * CH)

            def dense(s, m, c, rh, rl, kts=range(8), width=UC, r0=0):
                return (lambda bk: bk[:, 0:CH],
                        [(wh[s][:, kt * width + m * P:kt * width + m * P + P],
                          wl[s][:, kt * width + m * P:kt * width + m * P + P],
                          rh[:, kt - r0, chunk(c)], rl[:, kt - r0, chunk(c)]) for kt in kts])

            pe.wait_ge(S["consts"], 1)
            pe.wait_ge(S["small_in"], 16 * N_SMALL)
            pe.transpose(bank[0][:, 0:82], vecrow[:, :], ident[0:82, 0:82])
            for c in range(CB):
                mm = pe.transpose(bank[0][:, 96 + 16 * c:112 + 16 * c], histrow[:, c * P:(c + 1) * P], ident[0:16, 0:16])
            mm.then_inc(S["vec_turned"], 1)
            for kt in range(DB):
                mm = pe.transpose(bank[1][:, 9 * kt:9 * kt + 9], crow[:, kt * P:(kt + 1) * P], ident[0:9, 0:9])
            mm.then_inc(S["c_turned"], 1)

            def ada_pair(a_, before):
                for w in (0, 1):
                    pe.wait_ge(w_in(w), before * 32 + 32)
                    pe.wait_ge(S["mods_in"], a_ + (w - 1 + CREDIT))
                    v = raw[w][:, :].rearrange("p (k n) -> p k n", k=8)
                    for kt in range(DB):
                        mm = pe.matmul(bank[LIN[w]][0:9, 0:UC], cT[:, kt, :], v[:, kt, :], start=kt == 0, stop=kt == DB - 1)
                    mm.then_inc(S["ada_used"], 1)
                for w in (0, 1):
                    pe.wait_ge(S["ada_y"], a_ + (w + 1 + CREDIT))
                    for m in (0, 1):
                        at = UC + 9 * m
                        mm = pe.matmul(bank[LIN[w]][:, at:at + 9], adaY[w][:, m * P:(m + 1) * P], ident[0:9, 0:9],
                                       start=True, stop=True)
                    mm.then_inc(S["ada_turned"], 1)

            def feature_sums(acc_, n):
                pe.wait_ge(S["squares_added"], DB * (n + 1) + CREDIT)
                for c in range(NCH):
                    pe.matmul(bank[c][:, 0:CH], ones[:, :], acc_[:, chunk(c)], start=True, stop=True)\
                        .then_inc(S["squares_summed"], 1)

            def h_of(c, n):
                pe.wait_ge(S["h_lo"], n * H_PARTS + (DB * (c + 1) if c < NCH - 1 else H_PARTS))

            pe.wait_ge(S["c_ready"], 1)
            ada_pair(0, 0)
            pe.wait_ge(S["x_in"], 32)
            for t in range(9):
                rows = P if t < 8 else NS
                for half in (0, 1):
                    if t >= 2:
                        pe.wait_ge(S["xT_dve" if half else "xT_act"], t - 1)
                    for b in range(4):
                        mm = pe.transpose(bank[2 + 2 * (t % 2) + half][:, b * P:b * P + rows],
                                          xload[0:rows, t, (4 * half + b) * P:(4 * half + b + 1) * P],
                                          ident[0:rows, 0:rows])
                    mm.then_inc(S["x_turned"], 1)
            ada_pair(2, 1)
            pe.wait_ge(S["xT_act"], 9)
            pe.wait_ge(S["xT_dve"], 9)
            feature_sums(acc, 0)
            for a_ in range(4, ADA_FIRST, 2):
                ada_pair(a_, a_ // 2)
            pe.wait_ge(S["mods_in"], ADA_FIRST + CREDIT)

            def q_and_k(i, u):
                for m in (0, 1):
                    for c in range(NCH):
                        if u == 0 and m == 0:
                            h_of(c, 0)
                        yield dense(u, m, c, hH, hL)

            phase("qk", 2, q_and_k)

            def v_groups(i, u):
                for t in range(9):
                    n = P if t < 8 else NS
                    yield (lambda bk, n=n: bk[0:n, 0:UC],
                           [(hH[:, kt, t * P:t * P + n], hL[:, kt, t * P:t * P + n],
                             wh[u][:, kt * UC:(kt + 1) * UC], wl[u][:, kt * UC:(kt + 1) * UC]) for kt in range(DB)])

            phase("v", 2, v_groups)
            pe.wait_ge(S["bank_dve"], PHASES["conv"][1])
            with pe.Fori(0, 4) as i:
                for u in (0, 1):
                    pe.wait_ge(S["qk_square"], i * 2 + (u + 1))
                    pe.wait_ge(S["qk_rstd"], i * 2 + (CREDIT - 2 + u + 1))
                    for c in range(NCH):
                        mm = pe.matmul(bank[3 * u + c][:, 0:CH], headones[:, :], qsq[u][:, chunk(c)], start=True, stop=True)
                    mm.then_inc(S["qk_sum"], 1)
                    ada_pair(i * 4 + (ADA_FIRST + 2 * u), i * 2 + (7 + u))
            pe.wait_ge(S["mods_in"], ADA + CREDIT)
            pe.wait_ge(S["qk_ready"], 8 + CREDIT)
            for t in range(9):
                n = P if t < 8 else NS
                if t >= 2:
                    pe.wait_ge(S["kout_ready"], t - 1)
                for b in range(4):
                    mm = pe.transpose(bank[t % 2][0:n, b * P:(b + 1) * P], act8[:, 4 + b, t * P:t * P + n], ident[:, :])
                mm.then_inc(S["kturned"], 1)
            phase("conv", 2, lambda i, u: [dense(u, m, c, hH, hL) for m in (0, 1) for c in range(NCH)])
            phase("gates", 2, lambda i, u: [dense(u, m, c, hH, hL) for m in (0, 1) for c in range(NCH)])
            pe.wait_ge(S["yc_ready"], CB)
            for c in range(CB):
                mm = pe.transpose(bank[0][0:18, c * P:(c + 1) * P], tail[:, c, :], ident[:, :])
            mm.then_inc(S["tail_turned"], 1)

            def scores(p, u):
                qc, j, h, lo, _ = step_of(u)
                rows, keys, qs = slice(HD * h, HD * h + HD), slice(j * P, j * P + P), slice(512 * qc + lo, 512 * qc + 512)
                if u in (0, FIRST_LATE):
                    pe.wait_ge(S["pair_ready"], 2 * p + (1 + (u > 0)))
                pe.wait_ge(S["zb_done"], NSTEP * p + (u - 3 + CREDIT4))
                three(bank[(0, 1, 6, 7)[u % 4]][:, 0:512 - lo], [(kh[rows, keys], kl[rows, keys], qh[rows, qs], ql[rows, qs])])\
                    .then_inc(S["z_done"], 1)

            def block_sums(p, k):
                qc, j, h, lo, _ = step_of(k)
                pe.wait_ge(S["sp_lo"], NSTEP * p + (k + 1))
                if j == 4 * qc + 3:
                    pe.wait_ge(S["arg_done"], NSTEP * p + (k - 1 + CREDIT))
                out = bank[2 + h][:, lo:512]
                n = 512 - lo
                pe.matmul(out, suffix_r[:, :], sh[k % 4][:, 0:n], start=j == 4 * qc + 3, stop=False, skip_group_check=True)
                pe.matmul(out, suffix_r[:, :], sl[k % 4][:, 0:n], start=False, stop=j == 0,
                          skip_group_check=True).then_inc(S["tri_done"], 1)

            def rest_of_block(p, k):
                qc, j, h, lo, _ = step_of(k)
                if j == 0:
                    return
                out = bank[2 + h][:, lo:512]
                pe.wait_ge(S["arg_done"], NSTEP * p + (k + 1 + CREDIT))
                for x in (sh, sl):
                    pe.matmul(out, prefix_r[:, :], x[k % 4][:, 0:512 - lo], start=False, stop=False, skip_group_check=True)

            def values(p, k):
                qc, j, h, lo, _ = step_of(k)
                first = j == 4 * qc + 3
                n = 512 - lo
                if k in (0, FIRST_LATE):
                    pe.wait_ge(S["values_ready"], 2 * p + (1 + (k > 0)))
                pe.wait_ge(S["prob_lo"], NSTEP * p + (k + 1))
                if first:
                    pe.wait_ge(S["o_out"], 4 * p + (4 * (k // NSTEP) + 2 * qc + h - 1 + CREDIT))
                out = bank[4 + h][0:HD, lo:512]
                vH_, vL_ = (v[:, j, HD * h:HD * h + HD] for v in (vcH, vcL))
                pe.matmul(out, vH_, ph[k % 3][:, 0:n], start=first, stop=False, skip_group_check=True)
                pe.matmul(out, vL_, ph[k % 3][:, 0:n], start=False, stop=False, skip_group_check=True)
                pe.matmul(out, vH_, pl[k % 3][:, 0:n], start=False, stop=j == 0, skip_group_check=True)\
                    .then_inc(S["av_done"], 1)

            def prompt_steps(p, first=False, last=False):
                for u in range(NSTEP if not last else LATE_VALUES):
                    if u and not last:
                        scores(p, u)
                    for stage, late in ((block_sums, LATE_SUMS), (rest_of_block, LATE_REST), (values, LATE_VALUES)):
                        k = u - late
                        if (k >= 0 or not first) and (k < 0 or not last):
                            stage(p, k)
                    if u == 0 and not last:
                        scores(p, u)

            pe.wait_ge(S["tail_ready"], 1)
            pe.wait_ge(S["bank_act"], PHASES["mix"][2])
            prompt_steps(0, first=True)
            with pe.Fori(1, NPAIR) as p:
                prompt_steps(p)
            prompt_steps(NPAIR, last=True)

            def turn(b, n):
                c, pr = n // 4, n % 4
                if pr == 0:
                    pe.wait_ge(S[f"k_in{c}"], 64 * b + 64)
                pe.wait_ge(S["kt_lo"], 16 * b + (n - 1 + CREDIT))
                for g in range(4):
                    mm = pe.transpose(bank[n % 2][:, g * P:(g + 1) * P], kraw[c][:, g, pr * P:(pr + 1) * P], ident[:, :])
                mm.then_inc(S["kt_done"], 1)

            def score(b, n):
                c, pr = n // 4, n % 4
                pe.wait_ge(S["kt_lo"], 16 * b + (n + 1 + CREDIT))
                if n == 0:
                    pe.wait_ge(S["q_block"], b + 1)
                if pr == 0 and c < 2 and not (isinstance(b, int) and b == 0):
                    pe.wait_ge(S["zrow_ready"], 5 * b)
                if pr == 0 and c >= 2:
                    pe.wait_ge(S["zrow_ready"], 5 * b + (c - 1))
                out = bank[4 + c % 2][0:ROWS, :]
                qh_, ql_ = (q[:, pr * ROWS:(pr + 1) * ROWS] for q in (qbh, qbl))
                pe.matmul(out, qh_, kTh[:, pr, :], start=pr == 0, stop=False)
                pe.matmul(out, ql_, kTh[:, pr, :], start=False, stop=False)
                pe.matmul(out, qh_, kTl[:, pr, :], start=False, stop=pr == 3).then_inc(S["z_used"], 1)

            def score_new(b):
                pe.wait_ge(S["darg"], b + CREDIT)
                out = bank[3][0:ROWS, 128:128 + DEC_T]
                for pr in range(4):
                    qh_, ql_ = (q[:, pr * ROWS:(pr + 1) * ROWS] for q in (qbh, qbl))
                    pe.matmul(out, qh_, knh[:, pr, :], start=pr == 0, stop=False)
                    pe.matmul(out, ql_, knh[:, pr, :], start=False, stop=False)
                    mm = pe.matmul(out, qh_, knl[:, pr, :], start=False, stop=pr == 3)
                mm.then_inc(S["znew_done"], 1)

            def before_keys_down(b, c):
                pe.wait_ge(S["zrow_ready"], 5 * b + (c + 1 + (c == 3)))
                if c == 0:
                    pe.wait_ge(S["dabs"], b + CREDIT)

            def keys_down(b, c):
                for g in range(4):
                    page = 4 * c + g
                    mm = pe.transpose(bank[6][:, page * ROWS:(page + 1) * ROWS], zrow[:, g * P:(g + 1) * P],
                                      ident[0:ROWS, 0:ROWS])
                if c == 3:
                    mm = pe.transpose(bank[3][0:DEC_T, 64:64 + ROWS], zrow_new[:, :], ident[0:ROWS, 0:ROWS])
                mm.then_inc(S["dz_done"], 1)

            def suffix_sums(b):
                pe.wait_ge(S["dsum_ready"], b + 1)
                pe.wait_ge(S["darg"], b + CREDIT)
                if not (isinstance(b, int) and b == 0):
                    pe.wait_ge(S["d_oout"], b + CREDIT)
                o16, onew = bank[7][:, :], bank[3][:, 96:96 + ROWS]
                pe.matmul(onew, suffix_r[:, :], dsh[:, PAGES, :], start=True, stop=False)
                pe.matmul(onew, suffix_r[:, :], dsl[:, PAGES, :], start=False, stop=True)
                ops = ((suffix_r, dsh), (suffix_r, dsl), (ones_r, dch), (ones_r, dcl))
                for n, (w, r) in enumerate(ops):
                    mm = pe.matmul(o16, w[:, :], r[:, 0:PAGES, :].rearrange("p g c -> p (g c)"), start=n == 0, stop=n == 3)
                mm.then_inc(S["ds_done"], 1)

            def weigh_values(b, before_last=lambda: None):
                pe.wait_ge(S["dprob_lo"], b + 1)
                pe.wait_ge(S["d_osel"], b + CREDIT)
                for c in range(4):
                    pe.wait_ge(S["v_lo"], 4 * b + (c + 1))
                    if c == 3:
                        pe.wait_ge(S["vnew_lo"], b + 1)
                        before_last()
                    for g in range(4):
                        page = 4 * c + g
                        for v in (vh[c], vl[c]):
                            mm = pe.matmul(bank[2][0:2 * ROWS, :], dp2[:, page, :], v[:, g * ATT:(g + 1) * ATT],
                                           start=page == 0 and v is vh[c], stop=False)
                    mm.then_inc(S["d_av"], 1)
                pe.matmul(bank[2][0:2 * ROWS, :], dp2[0:DEC_T, PAGES, :], vnewH[:, :], start=False, stop=False)
                pe.matmul(bank[2][0:2 * ROWS, :], dp2[0:DEC_T, PAGES, :], vnewL[:, :], start=False, stop=True)\
                    .then_inc(S["d_av"], 1)

            def gather_heads(b):
                pe.wait_ge(S["d_osel"], b + (1 + CREDIT))
                pe.wait_ge(S["d_oout"], b + CREDIT)
                for pr in range(4):
                    mm = pe.matmul(bank[3][:, pr * 4:pr * 4 + 4], osel[:, pr * P:(pr + 1) * P], sel4[:, :],
                                   start=True, stop=True)
                mm.then_inc(S["d_otr"], 1)

            def sequence(b, prev=True, prev2=True):
                for n in range(18):
                    if n in (8, 12, 16):
                        before_keys_down(b, n // 4 - 2)
                    if n < 16:
                        turn(b, n)
                    if n >= 2:
                        score(b, n - 2)
                    if n in (8, 12, 16):
                        keys_down(b, n // 4 - 2)
                    if prev2 and n == 5:
                        gather_heads(b - 2)
                    if prev and n == 12:
                        suffix_sums(b - 1)
                score_new(b)
                if prev:
                    weigh_values(b - 1, lambda: before_keys_down(b, 3))
                else:
                    before_keys_down(b, 3)
                keys_down(b, 3)

            pe.wait_ge(S["o_out"], 4 * NPAIR + CREDIT)
            sequence(0, False, False)
            sequence(1, True, False)
            with pe.Fori(2, DEC_B) as b:
                sequence(b)
            gather_heads(DEC_B - 2)
            suffix_sums(DEC_B - 1)
            weigh_values(DEC_B - 1)
            gather_heads(DEC_B - 1)

            pe.wait_ge(S["d_oout"], DEC_B + CREDIT)

            def merge(i, u):
                for m in (0, 1):
                    for part in (0, 1):
                        for c in range(NCH):
                            if u == 0 and m == 0:
                                pe.wait_ge(S["oy_lo"], NCH * part + c + 1)
                            yield dense(u, m, c, *((oH, oL) if part == 0 else (ycH, ycL)),
                                        kts=range(4 * part, 4 * part + 4), r0=4 * part)

            phase("mix", 2, merge)
            pe.wait_ge(S["mix_lo"], 3 * DB + 3 * CREDIT)
            phase("wo", 2, lambda i, u: [dense(u, m, c, mixH, mixL) for m in (0, 1) for c in range(NCH)])
            feature_sums(acc2, 1)

            def mlp_groups(i, u):
                if u < 2:
                    for m in (0, 1):
                        for c in range(NCH):
                            if u == 0 and m == 0:
                                h_of(c, 1)
                            yield dense(u, m, c, h2H, h2L)
                    return
                for c in range(NCH):
                    if u == 2:
                        pe.wait_ge(S["hid_lo"], i * 12 + (10 + c))
                    for m in range(4):
                        yield dense(u % 2, m, c, hidH, hidL, kts=range(4), width=512)

            phase("mlp", 4, mlp_groups)
            pe.wait_ge(S["acc_done"], 1)
            for t in range(9):
                n = P if t < 8 else NS
                for half in (0, 1):
                    if t >= 2:
                        pe.wait_ge(S["y_dve" if half else "y_act"], t - 1)
                    for b in range(4):
                        mm = pe.transpose(bank[2 * (t % 2) + half][0:n, b * P:(b + 1) * P],
                                          x1[:, 4 * half + b, t * P:t * P + n], ident[:, :])
                    mm.then_inc(S["y_turned"], 1)

        @block.scalar
        def _(act):
            for n in ("bank_act", "mods_in", "qk_rstd", "prob_done", "o_out"):
                act.sem_inc(S[n], CREDIT)
            act.sem_inc(S["gate_dma0"], 16)
            act.sem_inc(S["gate_dma1"], 16)
            ch = Chain(act, S["act_step"])
            ev = act.activation

            def products(name, at, i=0):
                g, _, _, _, pattern = PHASES[name]
                act.wait_ge(S["products"], i * len(pattern) + (g + at + 1))

            act.preload_act_table_set("natural_log_exp_and_others")
            act.wait_ge(S["c_turned"], 1)
            ev(csig[:, :, :], bank[1][:, 0:9 * DB].rearrange("p (k c) -> p k c", k=DB), ACT.Exp, scale=-1.0)\
                .then_inc(S["c_exp"], 1)

            def mods_out(a_, w, i=0):
                act.wait_ge(S["ada_turned"], a_ + (w + 1 + CREDIT))
                cols_ = ds(a_ * 2 + 2 * w, 2) if not isinstance(a_, int) else slice(2 * (a_ + w), 2 * (a_ + w) + 2)
                ev(mods[:, cols_, :], bank[LIN[w]][:, UC:UC + 18].rearrange("p (m c) -> p m c", m=2), ACT.Copy)\
                    .then_inc(S["mods_in"], 1)

            for w in (0, 1):
                mods_out(0, w)
            for t in range(9):
                n = P if t < 8 else NS
                act.wait_ge(S["x_turned"], 2 * t + 1)
                ev(act8[:, 0:4, t * P:t * P + n], bank[2 + 2 * (t % 2)][:, 0:4 * P].rearrange("p (b c) -> p b c", b=4)[:, :, 0:n],
                   ACT.Copy).then_inc(S["xT_act"], 1)
            act.wait_ge(S["xT_dve"], 9)
            act.wait_ge(S["xT_act"], 9)
            act.dma_start(x_dram.rearrange("b p t -> p b t"), act8[:, :, :]).then_inc(S["x_saved"], 16)

            def square(src, sqt, b, u, n):
                act.wait_ge(S["squares_added"], b + (DB * n - 1 + CREDIT))
                ev(sqt[u][:, :], src[:, b, :], ACT.Square).then_inc(S["squares"], 1)

            def inverse_rms(rs, n):
                for c in range(NCH):
                    act.wait_ge(S["squares_summed"], NCH * n + c + 1)
                    part = rs[:, c * CH:(c + 1) * CH]
                    ch.did(ev(part, bank[c][:, 0:CH], ACT.Ln, scale=1.0 / D, bias=eps[:, :]))
                    ch.sync()
                    ev(part, part, ACT.Exp, scale=-0.5).then_inc(S["rstd_ready"], 1)

            def h_hi(sc, hs_, hi, shift, n):
                for k in range(DB * NCH):
                    c, b = k // DB, k % DB
                    act.wait_ge(S["scaled_ready"], n * H_PARTS + k + 1)
                    ev(hi[:, b, c * CH:(c + 1) * CH], sc[k % 3][:, :], ACT.Identity, bias=mods[:, shift + b, 0:1])\
                        .then_inc(S["h_hi"], 1)
                act.wait_ge(S["scaled_ready"], (n + 1) * H_PARTS)
                ev(hi[:, :, SEQ:T], hs_[:, :, :], ACT.Copy).then_inc(S["h_hi"], 1)

            for b in range(DB):
                square(act8, sq, b, b % 2, 0)
                if b == 5:
                    for w in (0, 1):
                        mods_out(2, w)
            inverse_rms(rstd, 0)
            for a_ in range(4, ADA_FIRST, 2):
                for w in (0, 1):
                    mods_out(a_, w)
            act.wait_ge(S["mods_ready"], 1)
            h_hi(scaled, hs, hH, 0, 0)
            act.wait_ge(S["bank_dve"], PHASES["v"][1])
            act.wait_ge(S["h_lo"], H_PARTS)
            with act.Fori(0, 4) as i:
                ch.enter(i, 6)
                for u in (0, 1):
                    act.wait_ge(S["qk_sum"], i * 2 + (CREDIT - 2 + u + 1))
                    ev(qsq[u][:, :], act8[:, i * 2 + u, :], ACT.Square).then_inc(S["qk_square"], 1)
                for u in (0, 1):
                    act.wait_ge(S["qk_sum"], i * 2 + (CREDIT + u + 1))
                    act.wait_ge(S["qk_ready"], i * 2 + (u + 1 - 2 + CREDIT))
                    for c in range(NCH):
                        ch.did(ev(qrs[u][:, c * CH:(c + 1) * CH], bank[3 * u + c][:, 0:CH], ACT.Ln, scale=1.0 / HD,
                                  bias=eps[:, :]))
                    ch.sync()
                    ev(qrs[u][:, :], qrs[u][:, :], ACT.Exp, scale=-0.5).then_inc(S["qk_rstd"], 1)
                    for w in (0, 1):
                        mods_out(i * 4 + (ADA_FIRST + 2 * u), w)
                ch.leave(4)
            act.wait_ge(S["bank_dve"], PHASES["conv"][1])
            act.dma_start(a["v_prompt"][0, 0].rearrange("(t p) h d -> p t (h d)", p=P), vsb[:, 0:8, :]).then_inc(S["v_out"], 16)
            act.dma_start(a["v_sample"][0].rearrange("b t h d -> (b t) (h d)"), vsb[0:NS, 8, :]).then_inc(S["v_out"], 16)
            kd = (S["kout_dma0"], S["kout_dma1"])
            for t in range(9):
                n = P if t < 8 else NS
                act.wait_ge(S["kturned"], t + 1)
                if t >= 2:
                    act.wait_ge(kd[t % 2], 16 * (t // 2))
                ev(kout[t % 2][0:n, :], bank[t % 2][0:n, :], ACT.Copy).then_inc(S["kout_ready"], 1)
                act.wait_ge(S["kout_ready"], t + 1)
                dst = a["k_prompt"][0, 0, t * P:(t + 1) * P].rearrange("t h d -> t (h d)") if t < 8 else \
                    a["k_sample"][0].rearrange("b t h d -> (b t) (h d)")
                act.dma_start(dst, kout[t % 2][0:n, :]).then_inc(kd[t % 2], 16)
            act.wait_ge(kd[0], 5 * 16)
            act.wait_ge(kd[1], 4 * 16)
            act.sem_inc(S["kout_free"], 1)

            gd = (S["gate_dma0"], S["gate_dma1"])

            def gate_exp(name, i, at, u, c):
                products(name, at + c, i)
                ev(gt[u][:, c * CH:(c + 1) * CH], bank[LIN[(at + c) % 2]][:, 0:CH], ACT.Exp, scale=-1.0)\
                    .then_inc(S["bank_act"], 1)

            def store_gate(u, block_):
                act.wait_ge(S["gate_ready"], block_ + 1)
                act.dma_start(gate_dram[ds(block_, 1), :, :].rearrange("o p t -> (o p) t"), gt[u][:, :]).then_inc(gd[u], 16)

            with act.Fori(0, CB) as i:
                act.wait_ge(gd[0], i * 16 + 16)
                for c in range(NCH):
                    gate_exp("conv", i, 9, 0, c)
                store_gate(0, i)
            act.wait_ge(S["yc_ready"], CB)

            def four_gates(i, first=False):
                for q in range(4):
                    u = q % 2
                    before = (0 if u else CB) + q // 2
                    act.wait_ge(gd[u], i * 32 + (16 * before + 16))
                    for c in range(NCH):
                        gate_exp("gates", i, 3 * q, u, c)
                        if c == 1 and not (first and q == 0):
                            store_gate(1 - u, i * 4 + (CB + q - 1))

            four_gates(0, first=True)
            with act.Fori(1, 3) as i:
                four_gates(i)
            store_gate(1, 2 * DB - 1)
            act.wait_ge(S["tail_ready"], 1)
            act.dma_start(a["conv_prompt"][0, 0], tailT[0:2, :]).then_inc(S["tail_dma"], 16)
            act.dma_start(a["conv_sample"][0].rearrange("b j c -> (b j) c"), tailT[2:18, :]).then_inc(S["tail_dma"], 16)
            act.wait_ge(gd[0], 16 * 10 + 16)
            act.wait_ge(gd[1], 16 * 6 + 16)
            act.wait_ge(S["tail_dma"], 32)

            act.wait_ge(S["products"], PHASES["mix"][0])

            def prompt_steps(p, first=False, last=False):
                for u in range(NSTEP if not last else LATE_OUT):
                    now = not last and u
                    if now:
                        logarithm(p, u)
                    for stage, late in ((softplus_hi, LATE_SOFTPLUS), (weights, LATE_PROB), (output, LATE_OUT)):
                        k = u - late
                        if (k >= 0 or not first) and (k < 0 or not last):
                            stage(p, k)
                    if u == 0 and not last:
                        if not first:
                            act.wait_ge(S["z_done"], NSTEP * p + CREDIT)
                        qk_half(p, 0)
                        logarithm(p, u)
                    if u == QK_SECOND and not last:
                        qk_half(p, 1)
                    if u == V_FIRST and not last:
                        if not first:
                            act.wait_ge(S["av_done"], NSTEP * p + AV_CREDIT)
                        ev(vcH[:, 0:4, :], vsb[:, 0:4, ds(p * P, P)], ACT.Copy).then_inc(S["values_hi"], 1)
                    if u == V_SECOND and not last:
                        ev(vcH[:, 4:8, :], vsb[:, 4:8, ds(p * P, P)], ACT.Copy).then_inc(S["values_hi"], 1)

            def qk_half(p, half):
                cols_ = slice(512 * half, 512 * half + 512)
                ch.did(ev(qh[:, cols_], act8[:, p, cols_], ACT.Copy))
                ev(kh[:, cols_], act8[:, p + NPAIR, cols_], ACT.Copy).then_inc(S["qk_hi"], 1)

            def logarithm(p, u):
                t = tl[u % 3][:, 0:512 - step_of(u)[3]]
                act.wait_ge(S["absz"], NSTEP * p + (u + 1))
                ch.did(ev(t, t, ACT.Exp))
                ch.sync()
                ev(t, t, ACT.Ln, bias=1.0).then_inc(S["log_done"], 1)

            def softplus_hi(p, k):
                n = 512 - step_of(k)[3]
                act.wait_ge(S["sp_done"], NSTEP * p + (k + 1))
                act.wait_ge(S["av_done"], NSTEP * p + (k - 5 + AV_CREDIT))
                ev(sh[k % 4][:, 0:n], sp_[k % 3][:, 0:n], ACT.Copy).then_inc(S["sp_hi"], 1)

            def weights(p, k):
                n = 512 - step_of(k)[3]
                act.wait_ge(S["arg_done"], NSTEP * p + (k + 1 + CREDIT))
                act.wait_ge(S["av_done"], NSTEP * p + (k - 2 + AV_CREDIT))
                ev(prob[k % 3][:, 0:n], zb[k % 6][:, 0:n], ACT.Exp).then_inc(S["prob_done"], 1)
                act.wait_ge(S["prob_done"], NSTEP * p + (k + 1 + CREDIT))
                ev(ph[k % 3][:, 0:n], prob[k % 3][:, 0:n], ACT.Copy).then_inc(S["prob_hi"], 1)

            def output(p, k):
                qc, j, h, _, _ = step_of(k)
                if j:
                    return
                act.wait_ge(S["av_done"], NSTEP * p + (k + 1 + AV_CREDIT))
                ev(oF[HD * h:HD * h + HD, p + k // NSTEP, 512 * qc:512 * qc + 512], bank[4 + h][0:HD, :], ACT.Copy)\
                    .then_inc(S["o_out"], 1)

            prompt_steps(0, first=True)
            ch.sync()
            with act.Fori(1, NPAIR) as p:
                ch.enter(p - 1, 2 + NSTEP)
                prompt_steps(p)
                ch.leave(NPAIR - 1)
            prompt_steps(NPAIR, last=True)

            HALF = 1024
            VALUE_STEPS = (0, 1, 4, 5, 8, 10, 12, 13)

            def values_hi(b, c, half):
                if half:
                    ev(vh[c][:, HALF:2 * HALF], raw[c % 2][:, HALF:2 * HALF], ACT.Copy).then_inc(S["v_hi"], 1)
                    return
                act.wait_ge(S[f"v_in{c % 2}"], 128 * b + 64 * (c // 2 + 1))
                if not (isinstance(b, int) and b == 0):
                    act.wait_ge(S["d_av"], 5 * b + (c + 1 - 5 + CREDIT4))
                ev(vh[c][:, 0:HALF], raw[c % 2][:, 0:HALF], ACT.Copy).then_inc(S["v_hi"], 1)

            def zrow_out(b, c):
                act.wait_ge(S["z_used"], 16 * b + (4 * c + 4 + CREDIT4))
                act.wait_ge(S["dz_done"], 4 * b + (c + CREDIT))
                ev(zrow[:, :], bank[4 + c % 2][0:ROWS, :], ACT.Copy).then_inc(S["zrow_ready"], 1)

            def sequence(b, now=True, prev=True):
                for n in range(16):
                    if now:
                        act.wait_ge(S["kt_done"], 16 * b + (n + 1 + CREDIT))
                        act.wait_ge(S["z_used"], 16 * b + (n - 3 + CREDIT4))
                        ev(kTh[:, n % 4, :], bank[n % 2][:, :], ACT.Copy).then_inc(S["kt_hi"], 1)
                    if now and n in (6, 10, 14):
                        zrow_out(b, n // 4 - 1)
                    if not prev:
                        continue
                    if n == 3:
                        act.wait_ge(S["dabs"], b + CREDIT)
                        ch.did(ev(dtl[:, :, :], dtl[:, :, :], ACT.Exp))
                        ch.sync()
                        ev(dtl[:, :, :], dtl[:, :, :], ACT.Ln, bias=1.0).then_inc(S["dlog"], 1)
                    if n in VALUE_STEPS:
                        values_hi(b - 1, VALUE_STEPS.index(n) // 2, VALUE_STEPS.index(n) % 2)
                    if n == 9:
                        act.wait_ge(S["dsp_done"], b)
                        ch.did(ev(dsh[:, :, :], dsp[:, :, :], ACT.Copy))
                        ev(dch[:, :, :], dcar[:, 0:PAGES, :], ACT.Copy).then_inc(S["dsp_hi"], 1)
                    if n == 10:
                        act.wait_ge(S["vnew_in"], 16 * b)
                        ev(vnewH[:, :], vnew[:, :], ACT.Copy).then_inc(S["vnew_hi"], 1)
                    if n == 14:
                        act.wait_ge(S["darg"], b + CREDIT)
                        if not (isinstance(b, int) and b == 1):
                            act.wait_ge(S["d_av"], 5 * b + (CREDIT4 - 5))
                        ch.did(ev(dpr[:, :, :], dpr[:, :, :], ACT.Exp))
                        ch.sync()
                        ev(dp2[:, :, 0:ROWS], dpr[:, :, :], ACT.Copy).then_inc(S["dprob"], 1)
                if now:
                    zrow_out(b, 3)
                    act.wait_ge(S["znew_done"], b + 1)
                    ev(zrow_new[:, :], bank[3][0:ROWS, 128:128 + DEC_T], ACT.Copy).then_inc(S["zrow_ready"], 1)

            sequence(0, prev=False)
            sequence(1)
            ch.sync()
            with act.Fori(2, DEC_B) as b:
                ch.enter(b - 2, 3)
                sequence(b)
                ch.leave(DEC_B - 2)
            sequence(DEC_B, now=False)

            act.wait_ge(S["d_oout"], DEC_B + CREDIT)
            act.wait_ge(S["o_out"], 4 * NPAIR + CREDIT)
            act.wait_ge(S["d_av"], 5 * DEC_B + CREDIT4)
            for hi, x in ((oH, oF), (ycH, yc)):
                for c in range(NCH):
                    cols_ = slice(c * CH, (c + 1) * CH)
                    ev(hi[:, :, cols_], x[:, :, cols_], ACT.Copy).then_inc(S["oy_hi"], 1)
            act.wait_ge(S["oy_lo"], 2 * NCH)
            with act.Fori(0, DB // 2) as i:
                for m in (0, 1):
                    for c in range(NCH):
                        act.wait_ge(S["mix_done"], i * 6 + (3 * m + c + 1))
                        ev(mixH[:, i * 2 + m, c * CH:(c + 1) * CH], ga[m][:, c * CH:(c + 1) * CH], ACT.Copy)\
                            .then_inc(S["mix_hi"], 1)
            act.wait_ge(S["products"], PHASES["wo"][0])
            act.dma_start(x1[:, :, :], x_dram.rearrange("b p t -> p b t")).then_inc(S["x_back"], 16)
            with act.Fori(0, 4) as i:
                for u in (0, 1):
                    act.wait_ge(S["x1_done"], i * 2 + (u + 1))
                    square(x1, sq2, i * 2 + u, u, 1)
            inverse_rms(rstd2, 1)
            h_hi(scaled2, hs2, h2H, 3 * DB, 1)
            act.wait_ge(S["h_lo"], 2 * H_PARTS)
            with act.Fori(0, 8) as i:
                for k in range(13):
                    if k < 12:
                        products("mlp", k, i)
                        act.wait_ge(S["sq_done"], i * 12 + (k - 1 + CREDIT))
                        ev(rel[k % 2][:, :], bank[LIN[k % 2]][:, 0:CH], ACT.Relu).then_inc(S["bank_act"], 1)
                    k2 = k - 1
                    if k2 >= 0:
                        m, c = k2 // 3, k2 % 3
                        act.wait_ge(S["sq_done"], i * 12 + (k2 + 1 + CREDIT))
                        ev(hidH[:, m, c * CH:(c + 1) * CH], rsq[k2 % 2][:, :], ACT.Copy).then_inc(S["hid_hi"], 1)
            for t in range(9):
                n = P if t < 8 else NS
                act.wait_ge(S["y_turned"], 2 * t + 1)
                ev(yrow[0:n, t, 0:512], bank[2 * (t % 2)][0:n, :], ACT.Copy).then_inc(S["y_act"], 1)

        @block.vector
        def _(dve):
            for n in ("bank_dve", "ada_y", "squares_added", "qk_ready", "arg_done", "kt_lo", "dabs", "darg", "d_osel", "d_oout", "sq_done"):
                dve.sem_inc(S[n], CREDIT)
            dve.sem_inc(S["zb_done"], CREDIT4)
            dve.sem_inc(S["mix_lo"], 3 * CREDIT)
            ch = Chain(dve, S["dve_step"])
            ts, tt, stt, cp = dve.tensor_scalar, dve.tensor_tensor, dve.scalar_tensor_tensor, dve.tensor_copy

            def f(t):
                return t.bitcast(F32)

            def step(inst):
                ch.did(inst)

            def products(name, at, i=0):
                g, _, _, _, pattern = PHASES[name]
                dve.wait_ge(S["products"], i * len(pattern) + (g + at + 1))

            def chunk(c):
                return slice(c * CH, (c + 1) * CH)

            dve.wait_ge(S["consts"], 1)
            step(cp(suffix_r[:, :], sfx_f[:, :]))
            step(cp(prefix_r[:, :], pfx_f[:, :]))
            step(cp(ones_r[:, :], ones[:, :]))
            step(dve.tensor_reduce(sel4[:, :], ident[0:64, 0:64].rearrange("p (h q) -> p q h", q=4), AX.X, ALU.add))
            dve.wait_ge(S["vec_turned"], 1)
            step(cp(vec[:, :], bank[0][:, 0:82]))
            step(cp(hist[:, :, :], bank[0][:, 96:160].rearrange("p (b c) -> p b c", b=CB)))
            dve.wait_ge(S["c_exp"], 1)
            step(ts(csig[:, :, :], csig[:, :, :], 1.0, None, ALU.add))
            ch.sync()
            step(dve.reciprocal(csig[:, :, :], csig[:, :, :]))
            ch.sync()
            tt(cT[:, :, :], bank[1][:, 0:9 * DB].rearrange("p (k c) -> p k c", k=DB), csig[:, :, :], ALU.mult)\
                .then_inc(S["c_ready"], 1)
            step(ts(gqk[:, 0:4], vec[:, 80:81].to_broadcast([P, 4]), 1.0 / float(np.sqrt(HD)), None, ALU.mult))
            step(cp(gqk[:, 4:8], vec[:, 81:82].to_broadcast([P, 4])))
            step(dve.memset(acc[:, :], 0.0))

            def ada_out(a_, w):
                dve.wait_ge(S["ada_used"], a_ + (w + 1))
                dve.wait_ge(S["ada_turned"], a_ + (w - 1 + CREDIT))
                cp(adaY[w][:, :], bank[LIN[w]][0:9, 0:UC]).then_inc(S["ada_y"], 1)

            for w in (0, 1):
                ada_out(0, w)
            for t in range(9):
                n = P if t < 8 else NS
                dve.wait_ge(S["x_turned"], 2 * t + 2)
                cp(act8[:, 4:8, t * P:t * P + n], bank[3 + 2 * (t % 2)][:, :].rearrange("p (b c) -> p b c", b=4)[:, :, 0:n])\
                    .then_inc(S["xT_dve"], 1)

            def add_squares(acc_, sqt, b, u, n):
                dve.wait_ge(S["squares"], b + (DB * n + 1))
                dve.wait_ge(S["squares_added"], b + (DB * n + CREDIT))
                tt(acc_[:, :], acc_[:, :], sqt[u][:, :], ALU.add).then_inc(S["squares_added"], 1)

            def finish_mods(units, m0, m1, scale_at, gain_at):
                dve.wait_ge(S["mods_in"], units + CREDIT)
                step(tt(mods[:, m0:m1, :], mods[:, m0:m1, :],
                        vec[:, m0:m1].unsqueeze(2).to_broadcast([P, m1 - m0, 9]), ALU.add))
                ch.sync()
                step(stt(mods[:, scale_at:scale_at + DB, :], mods[:, scale_at:scale_at + DB, :], 1.0,
                         vec[:, gain_at:gain_at + DB].unsqueeze(2).to_broadcast([P, DB, 9]), ALU.add, ALU.mult))
                ch.sync()
                dve.sem_inc(S["mods_ready"], 1)

            def per_sequence(col):
                return mods[:, col, 1:9].rearrange("p (o b) -> p o b", o=1).rearrange("p o b -> p (o b)")\
                    .unsqueeze(2).to_broadcast([P, DEC_B, DEC_T])

            def by_sequence(t):
                return t.rearrange("p (b t) -> p b t", b=DEC_B)

            def modulate(src, rs, sc, hs_, hi, lo, shift, n):
                gain = shift + DB
                for k in range(DB * NCH + 1):
                    if k < DB * NCH:
                        c, b = k // DB, k % DB
                        if b == 0:
                            dve.wait_ge(S["rstd_ready"], NCH * n + c + 1)
                        if k >= 3:
                            dve.wait_ge(S["h_lo"], n * H_PARTS + k - 2)
                        stt(sc[k % 3][:, :], src[:, b, chunk(c)], mods[:, gain + b, 0:1], rs[:, chunk(c)], ALU.mult, ALU.mult)\
                            .then_inc(S["scaled_ready"], 1)
                    if k:
                        c, b = (k - 1) // DB, (k - 1) % DB
                        dve.wait_ge(S["h_hi"], n * H_PARTS + k)
                        stt(lo[:, b, chunk(c)], sc[(k - 1) % 3][:, :], mods[:, shift + b, 0:1], f(hi[:, b, chunk(c)]),
                            ALU.add, ALU.subtract).then_inc(S["h_lo"], 1)
                by_b = hs_[:, :, :].rearrange("p k (b t) -> p k b t", b=DEC_B)

                def sample_mods(m0):
                    return mods[:, m0:m0 + DB, 1:9].unsqueeze(3).to_broadcast([P, DB, DEC_B, DEC_T])

                step(tt(hs_[:, :, :], src[:, :, samp], rs[:, samp].unsqueeze(1).to_broadcast([P, DB, NS]), ALU.mult))
                ch.sync()
                step(tt(by_b, by_b, sample_mods(gain), ALU.mult))
                ch.sync()
                tt(by_b, by_b, sample_mods(shift), ALU.add).then_inc(S["scaled_ready"], 1)
                dve.wait_ge(S["h_hi"], (n + 1) * H_PARTS)
                dve.wait_ge(S["h_lo"], (n + 1) * H_PARTS - 1)
                tt(lo[:, :, samp], hs_[:, :, :], f(hi[:, :, samp]), ALU.subtract).then_inc(S["h_lo"], 1)

            samp = slice(SEQ, T)
            ch.sync()
            for b in range(DB):
                add_squares(acc, sq, b, b % 2, 0)
                if b in (2, 4):
                    ada_out(2, (b - 2) // 2)
            for a_ in range(4, ADA_FIRST, 2):
                for w in (0, 1):
                    ada_out(a_, w)
            finish_mods(ADA_FIRST, 0, 2 * DB, DB, 48)
            modulate(act8, rstd, scaled, hs, hH, hL, 0, 0)

            dve.wait_ge(S["x_saved"], 16)
            dve.wait_ge(S["h_lo"], H_PARTS)
            with dve.Fori(0, 2) as i:
                for k in range(12):
                    products("qk", k, i)
                    cp(act8[:, i * 4 + k // 3, chunk(k % 3)], bank[LIN[k % 2]][:, 0:CH]).then_inc(S["bank_dve"], 1)
            for k in range(18):
                u, t = k // 9, k % 9
                n = P if t < 8 else NS
                products("v", k)
                cp(vsb[0:n, t, u * UC:(u + 1) * UC], bank[LIN[k % 2]][0:n, 0:UC]).then_inc(S["bank_dve"], 1)
            with dve.Fori(0, 4) as i:
                for u in (0, 1):
                    dve.wait_ge(S["qk_rstd"], i * 2 + (u + 1 + CREDIT))
                    b = i * 2 + u
                    stt(act8[:, b, :], act8[:, b, :], gqk[:, ds(b, 1)], qrs[u][:, :], ALU.mult, ALU.mult)\
                        .then_inc(S["qk_ready"], 1)
                    for w in (0, 1):
                        ada_out(i * 4 + (ADA_FIRST + 2 * u), w)
            finish_mods(ADA, 2 * DB, NMOD * DB, 4 * DB, 56)
            dve.wait_ge(S["kout_free"], 1)
            step(dve.memset(up[:, 0:2], 0.0))
            with dve.Fori(0, CB) as i:
                ch.enter(i, 11)
                for c in range(NCH):
                    products("conv", c, i)
                    cp(hcs[:, chunk(c)], bank[LIN[c % 2]][:, 0:CH]).then_inc(S["bank_dve"], 1)
                step(cp(us[:, :, 0:2], hist[:, ds(i, 1), :].rearrange("p o (b j) -> p (o b) j", j=2)))
                for c in range(NCH):
                    k = 3 + c
                    products("conv", k, i)
                    n = CH if c < 2 else LASTP
                    ps = bank[LIN[k % 2]]
                    if c == 0:
                        dve.wait_ge(S["bank_dve"], i * 9 + (PHASES["conv"][1] + 3))
                    one = tt(up[:, 2 + c * CH:2 + c * CH + n], ps[:, 0:n], hcs[:, c * CH:c * CH + n], ALU.mult)
                    if c == 2:
                        step(one)
                        one = tt(us[:, :, 2:6], by_sequence(ps[:, LASTP:CH]), by_sequence(hcs[:, samp]), ALU.mult)
                    one.then_inc(S["bank_dve"], 1)
                dve.wait_ge(S["bank_dve"], i * 9 + (PHASES["conv"][1] + 6))
                ch.sync()
                wt = [vec[:, ds(i + (64 + 4 * j), 1)] for j in range(3)]
                cb = vec[:, ds(i + 76, 1)]
                yp = yc[:, i, 0:SEQ]
                ysm = yc[:, i, samp].rearrange("p (b t) -> p b t", b=DEC_B)
                step(ts(yp, up[:, 0:SEQ], wt[0], cb, ALU.mult, ALU.add))
                step(ts(ysm, us[:, :, 0:4], wt[0], cb, ALU.mult, ALU.add))
                for j in (1, 2):
                    ch.sync()
                    step(stt(yp, up[:, j:j + SEQ], wt[j], yp, ALU.mult, ALU.add))
                    step(stt(ysm, us[:, :, j:j + 4], wt[j], ysm, ALU.mult, ALU.add))
                step(cp(tail[:, i, 0:2], up[:, SEQ:SEQ + 2]))
                step(cp(tail[:, ds(i, 1), 2:18].rearrange("p o (b j) -> p (o b) j", j=2), us[:, :, 4:6]))
                ch.sync()
                for c in range(NCH):
                    k = 6 + c
                    products("conv", k, i)
                    y = yc[:, i, chunk(c)]
                    tt(y, bank[LIN[k % 2]][:, 0:CH], y, ALU.mult).then_inc(S["bank_dve"], 1)
                dve.wait_ge(S["bank_act"], i * 3 + (PHASES["conv"][2] + 3))
                step(ts(gt[0][:, :], gt[0][:, :], 1.0, None, ALU.add))
                ch.sync()
                dve.reciprocal(gt[0][:, :], gt[0][:, :]).then_inc(S["gate_ready"], 1)
                ch.leave(CB)
            dve.wait_ge(S["bank_dve"], PHASES["gates"][1])
            dve.sem_inc(S["yc_ready"], CB)
            with dve.Fori(0, 3) as i:
                ch.enter(i, 4 * (2 * NCH - 1))
                for q in range(4):
                    for c in range(NCH):
                        part = gt[q % 2][:, chunk(c)]
                        dve.wait_ge(S["bank_act"], i * 12 + (PHASES["gates"][2] + 3 * q + c + 1))
                        step(ts(part, part, 1.0, None, ALU.add))
                        ch.sync()
                        one = dve.reciprocal(part, part)
                        if c < NCH - 1:
                            step(one)
                        else:
                            one.then_inc(S["gate_ready"], 1)
                ch.leave(3)
            dve.wait_ge(S["tail_turned"], 1)
            cp(tailT[:, :], bank[0][0:18, :]).then_inc(S["tail_ready"], 1)

            cp(qks[:, :, :], act8[:, :, SEQ:T]).then_inc(S["q_saved"], 1)

            def biased(p, u):
                qc, j, h, lo, diagonal = step_of(u)
                n = 512 - lo
                b = bias8[:, ds(p * 2 + h, 1)]
                z, o = bank[(0, 1, 6, 7)[u % 4]][:, 0:n], zb[u % 6][:, 0:n]
                dve.wait_ge(S["z_done"], NSTEP * p + (u + 1 + CREDIT))
                if u >= 6 or not isinstance(p, int):
                    dve.wait_ge(S["prob_done"], NSTEP * p + (u - 5 + CREDIT))
                if diagonal:
                    one = stt(o[:, 0:P], z[:, 0:P], b, diagcap[:, :], ALU.add, ALU.min)
                    if n > P:
                        step(one)
                        one = ts(o[:, P:n], z[:, P:n], b, None, ALU.add)
                else:
                    one = ts(o, z, b, None, ALU.add)
                one.then_inc(S["zb_done"], 1)
                dve.wait_ge(S["zb_done"], NSTEP * p + (u + 1 + CREDIT4))
                if u >= 3 or not isinstance(p, int):
                    dve.wait_ge(S["sp_done"], NSTEP * p + (u - 2))
                stt(tl[u % 3][:, 0:n], o, -1.0, o, ALU.mult, ALU.min).then_inc(S["absz"], 1)

            def softplus(p, k):
                n = 512 - step_of(k)[3]
                dve.wait_ge(S["log_done"], NSTEP * p + (k + 1))
                if k >= 3 or not isinstance(p, int):
                    dve.wait_ge(S["sp_lo"], NSTEP * p + (k - 2))
                stt(sp_[k % 3][:, 0:n], zb[k % 6][:, 0:n], 0.0, tl[k % 3][:, 0:n], ALU.max, ALU.add).then_inc(S["sp_done"], 1)

            def log_weight(p, k):
                _, _, h, lo, _ = step_of(k)
                o = zb[k % 6][:, 0:512 - lo]
                dve.wait_ge(S["tri_done"], NSTEP * p + (k + 1))
                tt(o, o, bank[2 + h][:, lo:512], ALU.subtract).then_inc(S["arg_done"], 1)

            def prompt_steps(p, first=False, last=False):
                for u in range(NSTEP if not last else LATE_SUMS):
                    if u and not last:
                        biased(p, u)
                    for stage, late in ((softplus, LATE_SOFTPLUS), (log_weight, LATE_SUMS)):
                        k = u - late
                        if (k >= 0 or not first) and (k < 0 or not last):
                            stage(p, k)
                    if u == 0 and not last:
                        qk_half(p, 0)
                        biased(p, u)
                    if u == QK_SECOND and not last:
                        qk_half(p, 1)
                    if u in (V_FIRST, V_SECOND) and not last:
                        half = int(u == V_SECOND)
                        js = slice(4 * half, 4 * half + 4)
                        dve.wait_ge(S["values_hi"], 2 * p + (half + 1))
                        tt(vcL[:, js, :], vsb[:, js, ds(p * P, P)], f(vcH[:, js, :]), ALU.subtract)\
                            .then_inc(S["values_ready"], 1)

            def qk_half(p, half):
                cols_ = slice(512 * half, 512 * half + 512)
                dve.wait_ge(S["qk_hi"], 2 * p + (half + 1))
                step(tt(ql[:, cols_], act8[:, p, cols_], f(qh[:, cols_]), ALU.subtract))
                tt(kl[:, cols_], act8[:, p + NPAIR, cols_], f(kh[:, cols_]), ALU.subtract).then_inc(S["pair_ready"], 1)

            prompt_steps(0, first=True)
            ch.sync()
            with dve.Fori(1, NPAIR) as p:
                ch.enter(p - 1, 2 + sum(1 for k in range(NSTEP) if step_of(k)[4] and step_of(k)[3] < 512 - P))
                prompt_steps(p)
                ch.leave(NPAIR - 1)
            prompt_steps(NPAIR, last=True)

            dve.wait_ge(S["v_out"], 32)
            dve.wait_ge(S["av_done"], AV_CREDIT + NPAIR * NSTEP)
            step(dve.memset(dzb[:, PAGES, :], NEG))
            step(dve.memset(qbF[:, :], 0.0))
            step(dve.memset(headmask[:, :, :], 1.0))
            step(cp(bias32[:, :, :], bias8[:, :].unsqueeze(2).to_broadcast([P, NH, DEC_T])))
            ch.sync()
            step(dve.tensor_tensor(headmask[:, :, :], headmask[:, :, :],
                                   headrow[:, :].unsqueeze(2).to_broadcast([2 * ROWS, NH, HD]), ALU.mult))
            ch.sync()

            def q_block(b):
                cols = ds(b * DEC_T, DEC_T)
                if not (isinstance(b, int) and b == 0):
                    dve.wait_ge(S["dz_done"], 4 * b + CREDIT)
                pair = qbF[:, :].rearrange("p (r x) -> p r x", x=40)
                step(cp(pair[0:HD, :, 0:4], qks[0:HD, 0:NPAIR, cols]))
                step(cp(pair[HD:P, :, 4:8], qks[HD:P, 0:NPAIR, cols]))
                step(cp(knh[:, :, :], qks[:, NPAIR:DB, cols]))
                ch.sync()
                step(cp(qbh[:, :], qbF[:, :]))
                step(tt(knl[:, :, :], qks[:, NPAIR:DB, cols], f(knh[:, :, :]), ALU.subtract))
                ch.sync()
                tt(qbl[:, :], qbF[:, :], f(qbh[:, :]), ALU.subtract).then_inc(S["q_block"], 1)

            def biased_scores(b, part):
                new = dzb[0:DEC_T, PAGES, :]
                if part:
                    ch.sync()
                    step(tt(new, new, newcap[:, :, :].rearrange("p h q -> p (h q)"), ALU.min))
                    ch.sync()
                    stt(dtl[:, :, :], dzb[:, :, :], -1.0, dzb[:, :, :], ALU.mult, ALU.min).then_inc(S["dabs"], 1)
                    return
                dve.wait_ge(S["dz_done"], 4 * b + (4 + CREDIT))
                b32 = bias32[:, :, :].rearrange("p h q -> p (h q)")
                step(tt(dzb[:, 0:PAGES, :], bank[6][:, :].rearrange("p (g c) -> p g c", g=PAGES),
                        b32.unsqueeze(1).to_broadcast([P, PAGES, ROWS]), ALU.add))
                step(tt(new, bank[3][0:DEC_T, 64:64 + ROWS], b32[0:DEC_T, :], ALU.add))

            def later_pages(b, part):
                for g in range(PAGES - 1 - 4 * part, PAGES - 5 - 4 * part, -1):
                    ch.sync()
                    one = cp(dcar[:, g, :], dsp[:, PAGES, :]) if g == PAGES - 1 else \
                        tt(dcar[:, g, :], dcar[:, g + 1, :], dsp[:, g + 1, :], ALU.add)
                    if g:
                        step(one)
                    else:
                        one.then_inc(S["dsp_done"], 1)

            def sequence(b, now=True, prev=True, prev2=True):
                for n in range(16):
                    if now:
                        dve.wait_ge(S["kt_hi"], 16 * b + (n + 1))
                        tt(kTl[:, n % 4, :], bank[n % 2][:, :], f(kTh[:, n % 4, :]), ALU.subtract).then_inc(S["kt_lo"], 1)
                        if n == 0:
                            q_block(b)
                    if prev and n == 1:
                        biased_scores(b - 1, 0)
                        biased_scores(b - 1, 1)
                    if prev2 and n == 3:
                        dve.wait_ge(S["d_av"], 5 * b + (5 - 10 + CREDIT4))
                        tt(osel[:, :], bank[2][0:2 * ROWS, :], headmask[:, :, :].rearrange("p h d -> p (h d)"), ALU.mult)\
                            .then_inc(S["d_osel"], 1)
                    if prev and n == 4:
                        dve.wait_ge(S["dlog"], b)
                        step(stt(dsp[:, :, :], dzb[:, :, :], 0.0, dtl[:, :, :], ALU.max, ALU.add))
                    if prev and 5 <= n < 9:
                        later_pages(b - 1, n - 5)
                    if prev2 and n == 9:
                        dve.wait_ge(S["d_otr"], b + (CREDIT - 1))
                        cp(oF[:, :, ds(b * DEC_T + (SEQ - 2 * DEC_T), DEC_T)],
                           bank[3][:, 0:16].rearrange("p (r q) -> p r q", r=4)).then_inc(S["d_oout"], 1)
                    if prev and n == 10:
                        dve.wait_ge(S["dsp_hi"], b)
                        step(tt(dsl[:, :, :], dsp[:, :, :], f(dsh[:, :, :]), ALU.subtract))
                        tt(dcl[:, :, :], dcar[:, 0:PAGES, :], f(dch[:, :, :]), ALU.subtract).then_inc(S["dsum_ready"], 1)
                    if prev and n == 13:
                        dve.wait_ge(S["ds_done"], b + CREDIT)
                        step(tt(dpr[:, 0:PAGES, :].rearrange("p g c -> p (g c)"),
                                dzb[:, 0:PAGES, :].rearrange("p g c -> p (g c)"), bank[7][:, :], ALU.subtract))
                        tt(dpr[:, PAGES, :], dzb[:, PAGES, :], bank[3][:, 96:96 + ROWS], ALU.subtract).then_inc(S["darg"], 1)
                    if prev and n == 15:
                        dve.wait_ge(S["dprob"], b)
                        tt(dp2[:, :, ROWS:2 * ROWS], dpr[:, :, :], f(dp2[:, :, 0:ROWS]), ALU.subtract)\
                            .then_inc(S["dprob_lo"], 1)

            sequence(0, prev=False, prev2=False)
            sequence(1, prev2=False)
            with dve.Fori(2, DEC_B) as b:
                ch.enter(b - 2, 26)
                sequence(b)
                ch.leave(DEC_B - 2)
            sequence(DEC_B, now=False)
            dve.wait_ge(S["d_av"], 5 * DEC_B + CREDIT4)
            tt(osel[:, :], bank[2][0:2 * ROWS, :], headmask[:, :, :].rearrange("p h d -> p (h d)"), ALU.mult)\
                .then_inc(S["d_osel"], 1)
            dve.wait_ge(S["d_otr"], DEC_B + CREDIT)
            cp(oF[:, :, T - DEC_T:T], bank[3][:, 0:16].rearrange("p (r q) -> p r q", r=4)).then_inc(S["d_oout"], 1)

            for n, (hi, lo, x) in enumerate(((oH, oL, oF), (ycH, ycL, yc))):
                for c in range(NCH):
                    dve.wait_ge(S["oy_hi"], n * NCH + c + 1)
                    tt(lo[:, :, chunk(c)], x[:, :, chunk(c)], f(hi[:, :, chunk(c)]), ALU.subtract).then_inc(S["oy_lo"], 1)
            with dve.Fori(0, 2) as i:
                for u in (0, 1):
                    for m in (0, 1):
                        b = 2 * u + m
                        dve.wait_ge(S[f"gates_in{m}"], i * 64 + 32 * (u + 1))
                        for part, g_ in ((0, ga[m]), (1, gb[m])):
                            for c in range(NCH):
                                k = 12 * u + 6 * m + 3 * part + c
                                products("mix", k, i)
                                tt(g_[:, chunk(c)], bank[LIN[k % 2]][:, 0:CH], g_[:, chunk(c)], ALU.mult)\
                                    .then_inc(S["bank_dve"], 1)
                        for c in range(NCH):
                            dve.wait_ge(S["bank_dve"], i * 24 + (PHASES["mix"][1] + 12 * u + 6 * m + 4 + c))
                            tt(ga[m][:, chunk(c)], ga[m][:, chunk(c)], gb[m][:, chunk(c)], ALU.add).then_inc(S["mix_done"], 1)
                        for c in range(NCH):
                            dve.wait_ge(S["mix_hi"], i * 12 + (3 * b + c + 1))
                            tt(mixL[:, i * 4 + b, chunk(c)], ga[m][:, chunk(c)], f(mixH[:, i * 4 + b, chunk(c)]), ALU.subtract)\
                                .then_inc(S["mix_lo"], 1)

            def gated_add(col, b, c, k):
                ps = bank[LIN[k % 2]]
                n = CH if c < 2 else LASTP
                x = x1[:, b, c * CH:c * CH + n]
                one = stt(x, ps[:, 0:n], mods[:, col, 0:1], x, ALU.mult, ALU.add)
                if c < 2:
                    one.then_inc(S["bank_dve"], 1)
                    return
                step(one)
                ch.sync()
                tt(by_sequence(smp[0][:, :]), by_sequence(ps[:, LASTP:CH]), per_sequence(col), ALU.mult)\
                    .then_inc(S["bank_dve"], 1)

            def sample_add(b):
                x = x1[:, b, samp]
                step(tt(x, x, smp[0][:, :], ALU.add))

            dve.wait_ge(S["x_back"], 16)
            step(dve.memset(acc2[:, :], 0.0))
            ch.sync()
            with dve.Fori(0, 2) as i:
                ch.enter(i, 4)
                for k in range(12):
                    b = i * 4 + k // 3
                    products("wo", k, i)
                    gated_add(b + 2 * DB, b, k % 3, k)
                    if k % 3 == 2:
                        dve.wait_ge(S["bank_dve"], i * 12 + (PHASES["wo"][1] + k + 1))
                        x = x1[:, b, samp]
                        tt(x, x, smp[0][:, :], ALU.add).then_inc(S["x1_done"], 1)
                        dve.wait_ge(S["x1_done"], i * 4 + (k // 3 + 1))
                        add_squares(acc2, sq2, b, (k // 3) % 2, 1)
                ch.leave(2)
            modulate(x1, rstd2, scaled2, hs2, h2H, h2L, 3 * DB, 1)
            dve.wait_ge(S["h_lo"], 2 * H_PARTS)
            with dve.Fori(0, 8) as i:
                ch.enter(i, 16)
                for k in range(12):
                    m, c = k // 3, k % 3
                    dve.wait_ge(S["bank_act"], i * 12 + (PHASES["mlp"][2] + k + 1))
                    tt(rsq[k % 2][:, :], rel[k % 2][:, :], rel[k % 2][:, :], ALU.mult).then_inc(S["sq_done"], 1)
                    dve.wait_ge(S["hid_hi"], i * 12 + (k + 1))
                    tt(hidL[:, m, chunk(c)], rsq[k % 2][:, :], f(hidH[:, m, chunk(c)]), ALU.subtract).then_inc(S["hid_lo"], 1)
                k = 12
                for u in (0, 1):
                    for c in range(NCH):
                        for m in range(4):
                            b = 4 * u + m
                            products("mlp", k, i)
                            if k == 12:
                                ch.sync()
                            gated_add(5 * DB + b, b, c, k)
                            if c == 2:
                                dve.wait_ge(S["bank_dve"], i * 24 + (PHASES["mlp"][1] + k - 12 + 1))
                                sample_add(b)
                            k += 1
                ch.leave(8)
            ch.sync()
            dve.wait_ge(S["bank_dve"], PHASES["mlp"][1] + 8 * 24)
            dve.sem_inc(S["acc_done"], 1)
            for t in range(9):
                n = P if t < 8 else NS
                dve.wait_ge(S["y_turned"], 2 * t + 2)
                cp(yrow[0:n, t, 512:D], bank[2 * (t % 2) + 1][0:n, :]).then_inc(S["y_dve"], 1)


IN_NAMES = ("x_prompt x_sample c_prompt c_sample cache_k cache_v state_conv page_table rms_g1 rms_g2 w_ada b_ada w_in "
            "q_norm_g k_norm_g sb_bias conv_w conv_b w_att_out w_conv_out w_o w_mlp1 w_mlp2").split()
OUTS = {
    "y_prompt": (1, SEQ, D), "y_sample": (DEC_B, DEC_T, D),
    "k_prompt": (1, 1, SEQ, NH, HD), "v_prompt": (1, 1, SEQ, NH, HD), "conv_prompt": (1, 1, 2, CONV),
    "k_sample": (1, DEC_B, DEC_T, NH, HD), "v_sample": (1, DEC_B, DEC_T, NH, HD), "conv_sample": (1, DEC_B, 2, CONV),
}


def kernel(**inputs):
    import concourse.bacc as bacc
    from concourse.bass_utils import run_bass_kernel_spmd

    nc = bacc.Bacc("TRN2", target_bir_lowering=False, num_devices=1)
    arrays, aps = {}, {}
    for name in IN_NAMES:
        arr = np.ascontiguousarray(inputs[name])
        arrays["in_" + name] = arr
        aps[name] = nc.dram_tensor("in_" + name, arr.shape, mybir.dt.from_np(arr.dtype), kind="ExternalInput").ap()
    for name, shape in OUTS.items():
        aps[name] = nc.dram_tensor("out_" + name, shape, F32, kind="ExternalOutput").ap()
    program(nc, aps)
    r = run_bass_kernel_spmd(nc, [arrays], core_ids=[0])
    return tuple(r.results[0]["out_" + name] for name in OUTS)
```
